# Optimizing a Trainium2 kernel written in Bass

```python
import jax, jax.numpy as jnp
from jax import lax
import numpy as np

D_MODEL = 2048
BATCH = 1
SEQ = 256
DEPTH = 1

N_META = 16
BLOCK = 128
PAD = BLOCK - N_META
EPS = 1e-6
NEG = -1e30

FOX_HEADS = 8
FOX_HEAD_DIM = D_MODEL // 16
FOX_WIDTH = FOX_HEADS * FOX_HEAD_DIM

CONV_CH = D_MODEL // 2
CONV_K = 3

GLA_HEADS = 4
GLA_DK = D_MODEL // 16
GLA_DV = D_MODEL // 8
GLA_RANK = 16
GLA_TAU = 16.0

D_FF = D_MODEL * 11 // 4
MLP_CONV_K = 3

SPLIT_SIZES = (FOX_WIDTH, FOX_WIDTH, FOX_WIDTH, FOX_HEADS,
               CONV_CH, CONV_CH, CONV_CH,
               GLA_HEADS * GLA_DK, GLA_HEADS * GLA_DK, GLA_HEADS * GLA_DV, GLA_HEADS * GLA_DV, GLA_RANK,
               D_MODEL, D_MODEL, D_MODEL)
N_IN = sum(SPLIT_SIZES)
SPLIT_POINTS = tuple(sum(SPLIT_SIZES[:i + 1]) for i in range(len(SPLIT_SIZES) - 1))
FOX_F_START = 3 * FOX_WIDTH

kernel_name = 'hybrid_fox_shortconv_gla_block'

def _rmsnorm(x, g):
    xf = x.astype(jnp.float32)
    y = xf * lax.rsqrt(jnp.mean(xf * xf, axis=-1, keepdims=True) + EPS)
    return (y * g.astype(jnp.float32)).astype(x.dtype)

def _causal_dwconv(x, w):
    k_width, ch = w.shape
    return lax.conv_general_dilated(x, w[:, None, :].astype(x.dtype), window_strides=(1,),
                                    padding=[(k_width - 1, 0)],
                                    dimension_numbers=('NWC', 'WIO', 'NWC'),
                                    feature_group_count=ch)

def _to_heads_padded(t, n_heads):
    b, l, w = t.shape
    t = t.reshape(b, l, n_heads, w // n_heads).transpose(0, 2, 1, 3)
    return jnp.pad(t, ((0, 0), (0, 0), (PAD, 0), (0, 0)))

def _from_heads_padded(t):
    b, h, lp, dh = t.shape
    return t[:, :, PAD:].transpose(0, 2, 1, 3).reshape(b, lp - PAD, h * dh)

def _fox_attention(q, k, v, logf):
    bn, nh, lp, dh = q.shape
    nb = lp // BLOCK
    c = jnp.cumsum(logf, axis=-1)
    pos = jnp.arange(lp)
    key_valid = pos >= PAD
    qb = jnp.moveaxis(q.reshape(bn, nh, nb, BLOCK, dh), 2, 0)
    cb = jnp.moveaxis(c.reshape(bn, nh, nb, BLOCK), 2, 0)
    scale = dh ** -0.5

    def one_block(args):
        qi, ci, i = args
        s = jnp.einsum('bhqd,bhkd->bhqk', qi, k, preferred_element_type=jnp.float32) * scale
        s = s + ci[..., None] - c[:, :, None, :]
        qpos = i * BLOCK + jnp.arange(BLOCK)
        mask = (pos[None, :] <= qpos[:, None]) & key_valid[None, :]
        p = jax.nn.softmax(jnp.where(mask, s, NEG), axis=-1)
        return jnp.einsum('bhqk,bhkd->bhqd', p.astype(v.dtype), v)

    out = lax.map(one_block, (qb, cb, jnp.arange(nb)))
    return jnp.moveaxis(out, 0, 2).reshape(bn, nh, lp, dh)

def _gla_chunked(q, k, v, logg):
    bn, nh, lp, dk = q.shape
    dv = v.shape[-1]
    nc = lp // BLOCK
    f32 = jnp.float32

    def to_chunks(t):
        return jnp.moveaxis(t.astype(f32).reshape(bn, nh, nc, BLOCK, t.shape[-1]), 2, 0)

    causal = jnp.tril(jnp.ones((BLOCK, BLOCK), dtype=bool))

    def step(state, inp):
        qc, kc, vc, gc = inp
        b = jnp.cumsum(gc, axis=2)
        diff = b[:, :, :, None, :] - b[:, :, None, :, :]
        decay = jnp.exp(jnp.where(causal[None, None, :, :, None], diff, -jnp.inf))
        att = jnp.einsum('bhtd,bhsd,bhtsd->bhts', qc, kc, decay)
        o = (jnp.einsum('bhts,bhsv->bhtv', att, vc)
             + jnp.einsum('bhtd,bhdv->bhtv', qc * jnp.exp(b), state))
        b_last = b[:, :, -1:, :]
        state = (jnp.exp(b_last[:, :, 0, :])[..., None] * state
                 + jnp.einsum('bhsd,bhsv->bhdv', kc * jnp.exp(b_last - b), vc))
        return state, o

    s0 = jnp.zeros((bn, nh, dk, dv), f32)
    _, o = lax.scan(step, s0, (to_chunks(q), to_chunks(k), to_chunks(v), to_chunks(logg)))
    return jnp.moveaxis(o, 0, 2).reshape(bn, nh, lp, dv)

def setup_inputs(seed: int = 0) -> dict:
    key = jax.random.key(seed)
    ks = jax.random.split(key, 20)

    def nrm(k, shape, scale):
        return jax.random.normal(k, shape, jnp.float32) * scale

    w_in = nrm(ks[3], (DEPTH, D_MODEL, N_IN), D_MODEL ** -0.5)
    w_in = w_in.at[:, :, FOX_F_START:FOX_F_START + FOX_HEADS].multiply(0.1)
    return {
        'x': nrm(ks[0], (BATCH, SEQ, D_MODEL), 1.0),
        'meta_tokens': nrm(ks[1], (N_META, D_MODEL), 1.0),
        'norm1_g': 1.0 + nrm(ks[2], (DEPTH, D_MODEL), 0.1),
        'w_in': w_in,
        'fox_b_f': 3.0 + nrm(ks[4], (DEPTH, FOX_HEADS), 0.1),
        'gate_b': nrm(ks[5], (DEPTH, 3 * D_MODEL), 0.01),
        'conv_w': nrm(ks[6], (DEPTH, CONV_K, CONV_CH), CONV_K ** -0.5),
        'gla_w_g2': nrm(ks[7], (DEPTH, GLA_RANK, GLA_HEADS * GLA_DK), GLA_RANK ** -0.5),
        'gla_b_g': nrm(ks[8], (DEPTH, GLA_HEADS * GLA_DK), 0.1),
        'gla_norm_g': 1.0 + nrm(ks[9], (DEPTH, GLA_HEADS * GLA_DV), 0.1),
        'w_a_o': nrm(ks[10], (DEPTH, FOX_WIDTH, D_MODEL), FOX_WIDTH ** -0.5),
        'w_b_o': nrm(ks[11], (DEPTH, CONV_CH, D_MODEL), CONV_CH ** -0.5),
        'w_c_o': nrm(ks[12], (DEPTH, GLA_HEADS * GLA_DV, D_MODEL), (GLA_HEADS * GLA_DV) ** -0.5),
        'w_o': nrm(ks[13], (DEPTH, D_MODEL, D_MODEL), D_MODEL ** -0.5),
        'norm2_g': 1.0 + nrm(ks[14], (DEPTH, D_MODEL), 0.1),
        'w_up': nrm(ks[15], (DEPTH, D_MODEL, 2 * D_FF), D_MODEL ** -0.5),
        'mlp_conv_w': nrm(ks[16], (DEPTH, MLP_CONV_K, 2 * D_FF), MLP_CONV_K ** -0.5),
        'w_down': nrm(ks[17], (DEPTH, D_FF, D_MODEL), D_FF ** -0.5),
        'final_norm_g': 1.0 + nrm(ks[18], (D_MODEL,), 0.1),
    }

def reference(x, meta_tokens, norm1_g, w_in, fox_b_f, gate_b, conv_w, gla_w_g2, gla_b_g,
              gla_norm_g, w_a_o, w_b_o, w_c_o, w_o, norm2_g, w_up, mlp_conv_w, w_down,
              final_norm_g):
    f32 = jnp.float32
    bn = x.shape[0]
    meta = jnp.broadcast_to(meta_tokens[None].astype(x.dtype), (bn, N_META, D_MODEL))
    h = jnp.concatenate([meta, x], axis=1)
    for l in range(DEPTH):
        xn = _rmsnorm(h, norm1_g[l])
        proj = xn @ w_in[l]
        (qa, ka, va, fa, sc_b, sc_c, sc_h, qc, kc, vc, rc, glr,
         g_a, g_b, g_c) = jnp.split(proj, SPLIT_POINTS, axis=-1)

        logf = jax.nn.log_sigmoid(fa.astype(f32) + fox_b_f[l].astype(f32))
        logf = jnp.pad(logf.transpose(0, 2, 1), ((0, 0), (0, 0), (PAD, 0)))
        oa = _fox_attention(_to_heads_padded(qa, FOX_HEADS), _to_heads_padded(ka, FOX_HEADS),
                            _to_heads_padded(va, FOX_HEADS), logf)
        ya = _from_heads_padded(oa) @ w_a_o[l]

        yb = (sc_b * _causal_dwconv(sc_c * sc_h, conv_w[l])) @ w_b_o[l]

        logg = jax.nn.log_sigmoid((glr @ gla_w_g2[l]).astype(f32) + gla_b_g[l].astype(f32)) / GLA_TAU
        oc = _gla_chunked(_to_heads_padded(qc * (GLA_DK ** -0.5), GLA_HEADS),
                          _to_heads_padded(kc, GLA_HEADS), _to_heads_padded(vc, GLA_HEADS),
                          _to_heads_padded(logg, GLA_HEADS))
        oc = _from_heads_padded(oc).astype(h.dtype)
        oc = _rmsnorm(oc.reshape(oc.shape[0], oc.shape[1], GLA_HEADS, GLA_DV),
                      gla_norm_g[l].reshape(GLA_HEADS, GLA_DV)).reshape(oc.shape)
        yc = (jax.nn.silu(rc) * oc) @ w_c_o[l]

        gbias = gate_b[l]
        mix = (jax.nn.sigmoid(g_a + gbias[:D_MODEL]) * ya
               + jax.nn.sigmoid(g_b + gbias[D_MODEL:2 * D_MODEL]) * yb
               + jax.nn.sigmoid(g_c + gbias[2 * D_MODEL:]) * yc)
        h = h + mix @ w_o[l]

        u = _causal_dwconv(_rmsnorm(h, norm2_g[l]) @ w_up[l], mlp_conv_w[l])
        u_gate, u_up = jnp.split(u, 2, axis=-1)
        h = h + (jax.nn.silu(u_gate) * u_up) @ w_down[l]
    return _rmsnorm(h, final_norm_g)[:, N_META:]


_drawn_inputs = setup_inputs


def setup_inputs(seed=0):
    import zlib

    import numpy as np

    out = dict(_drawn_inputs(seed))
    spreads = {}
    factors = {'fox_b_f': 50.656, 'gate_b': 24.155, 'gla_b_g': 4.522}
    for name, (base, spread) in spreads.items():
        noise = np.random.default_rng([zlib.crc32(name.encode()), seed]).standard_normal(out[name].shape)
        drawn = base * np.exp(spread * noise) if base else spread * noise
        out[name] = __import__('jax').numpy.asarray(drawn.astype(out[name].dtype))
    for name, factor in factors.items():
        out[name] = (out[name] * factor).astype(out[name].dtype)
    return out
```

```python
from contextlib import ExitStack

import concourse.bass as bass
from concourse import mybir

ALU = mybir.AluOpType
ACT = mybir.ActivationFunctionType
F32 = mybir.dt.float32
F32R = mybir.dt.float32r
AX_X = mybir.AxisListType.X

P = 128
EPS = 1e-6
NEG = -1e30
SLOTS = 4
LOOK = 3
KJ = 4
COLS = 256


class Phase:

    def __init__(self, prev, trips, segments):
        self.trips, self.n = trips, sum(segments)
        self.base = prev.base + prev.trips * prev.n if prev else 0
        self.land0 = [prev.land0[s] + prev.trips * prev.uses[s] for s in range(SLOTS)] if prev else [0] * SLOTS
        last = min(segments[-1], prev.segments[-1]) if prev else SLOTS
        self.segments = segments
        self.place = [(m, s) for m, length in enumerate(segments) for s in range(length)]
        self.back = [last if m == 0 else segments[m - 1] for m, _ in self.place]
        self.uses = [1 + sum(1 for length in segments if length > s) for s in range(SLOTS)]

    def wrap(self, i, q):
        return (i, q) if q < self.n else (i + 1, q - self.n)

    def slot(self, q):
        return self.place[q % self.n][1]

    def panel(self, i, q):
        return i * self.n + (self.base + q)

    def before(self, i, q):
        return self.panel(i, q) - self.back[q % self.n] + 1

    def landed(self, i, q):
        i, q = self.wrap(i, q)
        m, s = self.place[q]
        loads = 1 + sum(1 for length in self.segments[:m + 1] if length > s)
        return (i * self.uses[s]) * 16 + 16 * (self.land0[s] + loads)


def hybrid_layer(nc, x, meta_tokens, norm1_g, w_in, fox_b_f, gate_b, conv_w, gla_w_g2, gla_b_g,
                 gla_norm_g, w_a_o, w_b_o, w_c_o, w_o, norm2_g, w_up, mlp_conv_w, w_down,
                 final_norm_g, out):
    _, SEQ, D = x.shape
    META = meta_tokens.shape[0]
    T = META + SEQ
    KT = D // P
    FH = fox_b_f.shape[1]
    CONV_K, CH = conv_w.shape[1:]
    FW = w_a_o.shape[1]
    RANK, GK = gla_w_g2.shape[1:]
    GH = GK // P
    GV = w_c_o.shape[1]
    DFF = w_down.shape[1]
    FT = DFF // P
    BKT = FW // P
    Q0 = META - (CONV_K - 1)
    NQ = T - Q0
    C0 = Q0 - (CONV_K - 1)
    NC = T - C0
    SB = 16
    NSB = T // SB
    DV = GV // GH
    assert META == SB and SEQ == 2 * P and FW == CH == GV == 8 * P and DV == 2 * P and CONV_K == 3

    FOX_Q = 0
    FOX_K = FOX_Q + FW
    FOX_V = FOX_K + FW
    FOX_F = FOX_V + FW
    SC_B = FOX_F + FH
    SC_C = SC_B + CH
    SC_H = SC_C + CH
    GLA_Q = SC_H + CH
    GLA_K = GLA_Q + GK
    GLA_V = GLA_K + GK
    GLA_R = GLA_V + GV
    GLA_LR = GLA_R + GV
    GATES = GLA_LR + RANK

    PRO = Phase(None, 1, [4])
    BR = Phase(PRO, 4, [4] * 9)
    GT = Phase(BR, D // COLS, [4, 4, 4, 3, 3])
    WO = Phase(GT, D // COLS // 2, [4, 4])
    UP = Phase(WO, DFF // COLS, [4, 4])
    DN = Phase(UP, D // COLS // 2, [4, 4, 3, 4, 4, 3])
    BR_SET, BR_PER = (1, 1), (5, 4)
    GT_SET = tuple(BR_SET[s] + BR.trips * BR_PER[s] for s in range(2))
    WO_SET = tuple(GT_SET[s] + GT.trips * 3 for s in range(2))
    UP_SET = tuple(WO_SET[s] + WO.trips for s in range(2))
    DN_SET = tuple(UP_SET[s] + UP.trips for s in range(2))

    with ExitStack() as ctx:
        def sem(name):
            return ctx.enter_context(nc.semaphore(name))

        keep = ExitStack()

        def sb(name, shape, dt=F32, scope=None):
            return (scope or keep).enter_context(nc.sbuf_tensor(name, shape, dt))

        ps = ctx.enter_context(nc.psum_tensor("ps", [P, 8, 512], F32))
        AUX = [ps[:, 4 + b, :] for b in range(4)]

        def pset(s, n, rows=P):
            return ps[0:rows, 2 * s:2 * s + 2, 0:n]

        raw = sb("raw", [P, SLOTS, KJ * COLS])
        hi = sb("hi", [P, SLOTS, KJ * COLS], F32R)
        lo = sb("lo", [P, SLOTS, KJ * COLS], F32R)
        hT = sb("hT", [P, KT, T])
        par = sb("par", [P, 3 * KT + 3 * KT + 8 + GH])
        cvw = sb("cvw", [P, CONV_K, CH // P])
        mcw = sb("mcw", [P, CONV_K, 2 * FT])
        N1, N2, NF, GB, GN, BG = 0, KT, 2 * KT, 3 * KT, 6 * KT, 6 * KT + 8
        NPAR = BG + GH
        ident = sb("ident", [P, P])
        ones = sb("ones", [P, P])
        sqsum = sb("sqsum", [P, T])
        var = sb("var", [P, T])
        newt = sb("newt", [P, T])
        rinv = newt
        rstd = sb("rstd", [P, T])
        tokst = sb("tokst", [P, 4, 2])
        wg2 = sb("wg2", [RANK, GK])
        bf = sb("bf", [FH, 1])

        xn_scope = ExitStack()
        xh = sb("xh", [P, KT, T], F32R, xn_scope)
        xl = sb("xl", [P, KT, T], F32R, xn_scope)

        br_out = ExitStack()
        bo_h = sb("bo_h", [P, 3, BKT, NQ], F32R, br_out)
        bo_l = sb("bo_l", [P, 3, BKT, NQ], F32R, br_out)

        tmp = ExitStack()
        xa = sb("xa", [META, D], F32, tmp)
        xb = sb("xb", [P, 2, D], F32, tmp)
        prow = sb("prow", [P, 5, P], F32, tmp)
        xf = sb("xf", [P, 2, T], F32, tmp)
        sq1 = sb("sq1", [P, 4, T], F32, tmp)
        tmp.close()
        brt = ExitStack()
        ball = sb("ball", [P, GH, T], F32, brt)
        crow = sb("crow", [FH, T], F32, brt)
        ctok = sb("ctok", [P, 2, FH], F32, brt)
        ctok0 = sb("ctok0", [META, FH], F32, brt)
        causal = sb("causal", [P, P], F32, brt)
        blockd = sb("blockd", [P, T], F32, brt)
        every = sb("every", [P, P + SB], F32, brt)
        fv = sb("fv", [P, 2, T], F32, brt)
        fk = sb("fk", [P, 2, T], F32, brt)
        fq = sb("fq", [P, 2, T], F32, brt)
        gqk = sb("gqk", [P, 2, T], F32, brt)
        gv = sb("gv", [P, 2, T], F32, brt)
        cneg = sb("cneg", [FH, 2, T], F32, brt)
        vtok = sb("vtok", [P, 2, 2, P], F32, brt)
        vtok0 = sb("vtok0", [META, 2, P], F32, brt)
        nmax = sb("nmax", [P, 2, 3], F32, brt)
        psum_row = sb("psum_row", [P, 2, 3], F32, brt)
        pinv = sb("pinv", [P, 2, 3], F32, brt)
        bh = sb("bh", [P, T], F32, brt)
        eb = sb("eb", [P, T], F32, brt)
        qh = sb("qh", [P, 2, 7, SB], F32, brt)
        kd = sb("kd", [P, META + P], F32, brt)
        qe = sb("qe", [P, T], F32, brt)
        kdtok = sb("kdtok", [P, P], F32, brt)
        kdtok0 = sb("kdtok0", [META, P], F32, brt)
        gvt = sb("gvt", [P, 2, DV], F32, brt)
        gvt0 = sb("gvt0", [META, DV], F32, brt)
        att = sb("att", [P, T], F32, brt)
        state = sb("state", [P, 2, DV], F32, brt)
        cc, ch, cb = fv[:, :, 0:NC], fk[:, :, 0:NC], fq[:, :, 0:NQ]
        gr = gv[:, :, 0:NQ]
        on = cy = gqk[:, :, 0:NQ]
        early = ExitStack()
        NTRI = NSB * (SB * (SB + 1) // 2)
        tri = sb("tri", [P, NTRI], F32, early)
        kh = sb("kh", [P, 2, 7, P], F32, early)
        early.close()
        late = ExitStack()
        sc = sb("sc", [P, 2, 432], F32, late)
        pt = sb("pt", [P, 384], F32, late)
        pt0 = sb("pt0", [META, T], F32, late)
        osq = sb("osq", [P, 2, NQ], F32, late)
        sil = osq
        late.close()
        pro = ExitStack()
        zall = sb("zall", [P, GH, T], F32, pro)
        lall = sb("lall", [P, GH, T], F32, pro)
        flog = sb("flog", [FH, 3, T], F32, pro)
        onesT = sb("onesT", [P, T], F32, pro)
        glr = sb("glr", [RANK, T], F32, pro)
        pro.close()
        brt.close()
        gtt = ExitStack()
        mix_h = sb("mix_h", [P, KT, NQ], F32R, gtt)
        mix_l = sb("mix_l", [P, KT, NQ], F32R, gtt)
        gate = sb("gate", [P, 3, 2, NQ], F32, gtt)
        mixf = sb("mixf", [P, 2, NQ], F32, gtt)
        mixt = sb("mixt", [P, 2, NQ], F32, gtt)
        osqm = sb("osqm", [P, 2, NQ], F32, gtt)
        gtt.close()
        br_out.close()
        upt = ExitStack()
        act_h = sb("act_h", [P, FT, SEQ], F32R, upt)
        act_l = sb("act_l", [P, FT, SEQ], F32R, upt)
        uu = sb("uu", [P, 2, NQ], F32, upt)
        yg = sb("yg", [P, 2, SEQ], F32, upt)
        yu = sb("yu", [P, 2, SEQ], F32, upt)
        upt.close()
        xn_scope.close()
        ybuf = sb("ybuf", [P, 2, D])
        h3 = sb("h3", [P, 2, SEQ])
        hg = sb("hg", [P, 2, SEQ])
        sq3 = sb("sq3", [P, 2, SEQ])

        landed = [sem(f"landed{s}") for s in range(SLOTS)]
        hi_ready = sem("hi_ready")
        lo_ready = sem("lo_ready")
        panel_used = sem("panel_used")
        set_free = [sem("set0_free"), sem("set1_free")]
        vec = sem("vec")
        x_in = [sem(f"x_in{b}") for b in range(3)]
        par_in = sem("par_in")
        small_in = sem("small_in")
        sp_turn = sem("sp_turn")
        const_set = sem("const_set")
        raw_zero = sem("raw_zero")
        par_t, par_ok = sem("par_t"), sem("par_ok")
        xt_ps, xt_copied, xt_squared, xsq_sum = sem("xt_ps"), sem("xt_copied"), sem("xt_squared"), sem("xsq_sum")
        stat_ps, stat_inv, stat_root = sem("stat_ps"), sem("stat_inv"), sem("stat_root")
        xn_full, xn_hi, xn_lo = sem("xn_full"), sem("xn_hi"), sem("xn_lo")
        glr_copied = sem("glr_copied")
        z_ps, z_copied, z_neg, z_exp, z_one, z_log = (sem(n) for n in ("z_ps", "z_copied", "z_neg", "z_exp", "z_one", "z_log"))
        b_ready = sem("b_ready")
        c_ready, ctok_ps, ctok_copied = sem("c_ready"), sem("ctok_ps"), sem("ctok_copied")
        bh_ready, eb_ready = sem("bh_ready"), sem("eb_ready")
        tri_sub, off_sub, tri_exp, off_exp = sem("tri_sub"), sem("off_sub"), sem("tri_exp"), sem("off_exp")
        kd_ready, off_ready, tri_ready, qe_ready = sem("kd_ready"), sem("off_ready"), sem("tri_ready"), sem("qe_ready")
        kd_ps, kdtok_ready, gv_ps, gvt_ready = sem("kd_ps"), sem("kdtok_ready"), sem("gv_ps"), sem("gvt_ready")
        off_ps, tri_ps, st0_ps, st1_ps = sem("off_ps"), sem("tri_ps"), sem("st0_ps"), sem("st1_ps")
        st0_ready, st1_ready, att_ready, go_ps, go_copied = (sem(n) for n in ("st0_ready", "st1_ready", "att_ready", "go_ps", "go_copied"))
        gstat_ps, gstat_inv, gstat_root = sem("gstat_ps"), sem("gstat_inv"), sem("gstat_root")
        cneg_ready, vt_ps, vtok_ready, score_ps = sem("cneg_ready"), sem("vt_ps"), sem("vtok_ready"), sem("score_ps")
        smax_ready, p_exp, p_ready, pt_ps, pt_copied, pv_ps = (sem(n) for n in ("smax_ready", "p_exp", "p_ready", "pt_ps", "pt_copied", "pv_ps"))
        r_neg, r_exp, oc_full, oc_hi, oa_hi, ob_full, ob_hi, bo_lo = (sem(n) for n in ("r_neg", "r_exp", "oc_full", "oc_hi", "oa_hi", "ob_full", "ob_hi", "bo_lo"))
        mix_full, mix_hi, mix_lo = sem("mix_full"), sem("mix_hi"), sem("mix_lo")
        h2_hi, h2_lo, h2_squared, h2sq_sum = (sem(n) for n in ("h2_hi", "h2_lo", "h2_squared", "h2sq_sum"))
        r2_ps, r2_step, r2_inv, r2_root = sem("r2_ps"), sem("r2_step"), sem("r2_inv"), sem("r2_root")
        gate_conv, gate_silu, act_full, act_hi, act_lo = (sem(n) for n in ("gate_conv", "gate_silu", "act_full", "act_hi_ok", "act_lo_ok"))
        h3_scaled, h3_squared, yt_ps, yt_copied = (sem(n) for n in ("h3_scaled", "h3_squared", "yt_ps", "yt_copied"))
        fst_sum, fst_ps, fst_inv, fst_root, y_scaled, y_out = (sem(n) for n in ("fst_sum", "fst_ps", "fst_inv", "fst_root", "y_scaled", "y_out"))

        def panel(buf, s):
            return buf[:, s, :].rearrange("p (j n) -> p j n", j=KJ)

        def tiles(buf, s, j, n):
            return buf[:, s, j * COLS + n * P:j * COLS + (n + 1) * P]

        tri_at = [NSB * sum(SB - u for u in range(r)) for r in range(SB)]

        def tri_r(r):
            return tri[:, tri_at[r]:tri_at[r] + NSB * (SB - r)].rearrange("p (i t) -> p i t", i=NSB)

        def subs(row):
            return row.rearrange("p (i t) -> p i t", t=SB)

        def chunks(row):
            return row[:, META:T].rearrange("p (c t) -> p c t", c=2)

        def chunk_subs(row):
            return row[:, META:T].rearrange("p (c i t) -> p c i t", c=2, t=SB)

        wi = w_in[0]

        block = ctx.enter_context(nc.Block())

        @block.sync
        def _(sp):
            sp.dma_start(xa[:], meta_tokens).then_inc(x_in[0], 16)
            for b in range(2):
                sp.dma_start(xb[:, b, :], x[0, b * P:(b + 1) * P, :]).then_inc(x_in[1 + b], 16)
            for at, src, rows in ((N1, norm1_g[0], KT), (N2, norm2_g[0], KT), (NF, final_norm_g, KT),
                                  (GB, gate_b[0], 3 * KT), (GN, gla_norm_g[0], 8), (BG, gla_b_g[0], GH)):
                sp.dma_start(prow[at:at + rows, 0, :], src.rearrange("(a b) -> a b", b=P)).then_inc(par_in, 16)
            sp.dma_start(prow[0:CONV_K * CH // P, 1, :], conv_w[0].rearrange("k (a b) -> (k a) b", b=P)).then_inc(par_in, 16)
            for k in range(CONV_K):
                sp.dma_start(prow[0:2 * FT, 2 + k, :], mlp_conv_w[0, k].rearrange("(a b) -> a b", b=P)).then_inc(par_in, 16)
            sp.dma_start(wg2[:], gla_w_g2[0]).then_inc(small_in, 16)
            sp.dma_start(bf[:], fox_b_f[0].rearrange("(a b) -> a b", b=1)).then_inc(small_in, 16)
            sp.wait_ge(raw_zero, 1)
            for s in range(SLOTS):
                rows = wi[s * KJ * P:(s + 1) * KJ * P, :]
                sp.dma_start(panel(raw, s)[:, :, 0:FH],
                             rows[:, FOX_F:FOX_F + FH].rearrange("(j p) n -> p j n", p=P)).then_inc(landed[s], 16)
                sp.dma_start(panel(raw, s)[:, :, P:P + RANK],
                             rows[:, GLA_LR:GLA_LR + RANK].rearrange("(j p) n -> p j n", p=P)).then_inc(landed[s], 16)

            def load(ph, i, q, w, k0, col):
                sp.wait_ge(lo_ready, ph.before(i, q))
                if k0 == 0:
                    sp.sem_inc(sp_turn, 1)
                s = ph.slot(q)
                parts = 2 if q < SLOTS else 1
                kts = KJ // parts
                for j in range(0, KJ, kts):
                    sp.dma_start(panel(raw, s)[:, j:j + kts, :],
                                 w[(k0 + j) * P:(k0 + j + kts) * P, bass.ds(col, COLS)].rearrange("(j p) n -> p j n", p=P)
                                 ).then_inc(landed[s], 16)

            with sp.Fori(0, BR.trips) as i:
                for q in range(4):
                    sp.wait_ge(lo_ready, BR.before(i, q))
                    s = BR.slot(q)
                    for n, col in enumerate((GLA_Q, GLA_K)):
                        sp.dma_start(panel(raw, s)[:, :, n * P:(n + 1) * P],
                                     wi[q * KJ * P:(q + 1) * KJ * P, bass.ds(i * P + col, P)]
                                     .rearrange("(j p) n -> p j n", p=P)).then_inc(landed[s], 16)
                for p_, col in enumerate((GLA_V, FOX_V, FOX_K, FOX_Q, GLA_R, SC_C, SC_H, SC_B)):
                    for q in range(4):
                        load(BR, i, 4 * (p_ + 1) + q, wi, q * KJ, i * COLS + col)
            with sp.Fori(0, GT.trips) as i:
                for g in range(3):
                    for q in range(4):
                        load(GT, i, 4 * g + q, wi, q * KJ, i * COLS + (GATES + g * D))
                for g, w in enumerate((w_a_o, w_b_o, w_c_o)):
                    for q in range(2):
                        load(GT, i, 12 + 2 * g + q, w[0], q * KJ, i * COLS)
            with sp.Fori(0, WO.trips) as i:
                for q in range(8):
                    load(WO, i, q, w_o[0], (q % 4) * KJ, i * (2 * COLS) + (q // 4) * COLS)
            with sp.Fori(0, UP.trips) as i:
                for q in range(8):
                    load(UP, i, q, w_up[0], (q % 4) * KJ, i * COLS + (q // 4) * DFF)
            with sp.Fori(0, DN.trips) as i:
                for q in range(22):
                    load(DN, i, q, w_down[0], (q % 11) * KJ, i * (2 * COLS) + (q // 11) * COLS)
            for b in range(2):
                for h in range(2):
                    sp.wait_ge(y_scaled, 2 * b + h + 1)
                    sp.dma_start(out[0, b * P:(b + 1) * P, h * (D // 2):(h + 1) * (D // 2)],
                                 ybuf[:, b, h * (D // 2):(h + 1) * (D // 2)]).then_inc(y_out, 16)
            sp.wait_ge(y_out, 64)

        @block.gpsimd
        def _(pool):
            nc.gpsimd.memset(ident[:], 0.0).then_inc(const_set, 1)
            pool.wait_ge(const_set, 1)
            nc.gpsimd.affine_select(out=ident[:], in_=ident[:], compare_op=ALU.not_equal, fill=1.0, base=0,
                                    pattern=[[-1, P]], channel_multiplier=1).then_inc(const_set, 1)
            nc.gpsimd.memset(raw[:], 0.0).then_inc(raw_zero, 1)
            nc.gpsimd.memset(ones[:], 1.0).then_inc(const_set, 1)
            pool.wait_ge(const_set, 3)
            for kt in range(KT):
                pool.wait_ge(xt_squared, kt + 1)
                if kt == 0:
                    nc.gpsimd.tensor_copy(sqsum[:], sq1[:, 0, :]).then_inc(xsq_sum, 1)
                else:
                    pool.wait_ge(xsq_sum, kt)
                    nc.gpsimd.tensor_tensor(sqsum[:], sqsum[:], sq1[:, kt % 4, :], ALU.add).then_inc(xsq_sum, 1)
            pool.wait_ge(xn_lo, KT)
            nc.gpsimd.memset(causal[:], 0.0).then_inc(const_set, 1)
            nc.gpsimd.memset(blockd[:], 1.0).then_inc(const_set, 1)
            pool.wait_ge(const_set, 5)
            nc.gpsimd.affine_select(out=causal[:], in_=causal[:], compare_op=ALU.is_ge, fill=NEG, base=0,
                                    pattern=[[-1, P]], channel_multiplier=1).then_inc(const_set, 1)
            nc.gpsimd.affine_select(out=blockd[:, 0:META], in_=blockd[:, 0:META], compare_op=ALU.is_ge, fill=0.0, base=SB - 1,
                                    pattern=[[0, META]], channel_multiplier=-1).then_inc(const_set, 1)
            bd = chunk_subs(blockd[:])
            nc.gpsimd.affine_select(out=bd, in_=bd, compare_op=ALU.is_ge, fill=0.0, base=0,
                                    pattern=[[0, 2], [-SB, 8], [0, SB]], channel_multiplier=1).then_inc(const_set, 1)
            pool.wait_ge(const_set, 8)
            nc.gpsimd.affine_select(out=bd, in_=bd, compare_op=ALU.is_ge, fill=0.0, base=SB - 1,
                                    pattern=[[0, 2], [SB, 8], [0, SB]], channel_multiplier=-1).then_inc(const_set, 1)

        @block.scalar
        def _(act):
            def round_panel(ph, i, q):
                s = ph.slot(q)
                act.wait_ge(landed[s], ph.landed(i, q))
                act.wait_ge(panel_used, ph.before(i, q))
                nc.scalar.copy(hi[:, s, :], raw[:, s, :]).then_inc(hi_ready, 1)

            def pair_done(ph, i, q):
                act.wait_ge(panel_used, ph.panel(i, q) + 1)

            for kt in range(KT):
                act.wait_ge(xt_copied, kt + 1)
                if kt >= 4:
                    act.wait_ge(xsq_sum, kt - 3)
                nc.scalar.activation(sq1[:, kt % 4, :], hT[:, kt, :], ACT.Square).then_inc(xt_squared, 1)
            act.wait_ge(par_t, 1)
            nc.scalar.copy(par[:], ps[:, 2, 0:NPAR]).then_inc(par_ok, 1)
            nc.scalar.copy(cvw[:].rearrange("p k a -> p (k a)"), ps[:, 2, P:P + CONV_K * CH // P]).then_inc(par_ok, 1)
            nc.scalar.copy(mcw[:].rearrange("p k a -> p (k a)"), ps[:, 3, 0:CONV_K * 2 * FT]).then_inc(par_ok, 1)
            for q in range(4):
                act.wait_ge(landed[q], 32)
                nc.scalar.copy(hi[:, q, :], raw[:, q, :]).then_inc(hi_ready, 1)
            act.wait_ge(stat_inv, 1)
            nc.scalar.activation(rstd[:], rinv[:], ACT.Sqrt).then_inc(stat_root, 1)
            for kt in range(KT):
                act.wait_ge(xn_full, kt + 1)
                nc.scalar.copy(xh[:, kt, :], xf[:, kt % 2, :]).then_inc(xn_hi, 1)
            for q in range(LOOK):
                round_panel(BR, 0, q)
            act.wait_ge(panel_used, 4)
            nc.scalar.copy(glr[:], ps[0:RANK, 1, 0:T]).then_inc(glr_copied, 1)
            act.wait_ge(z_neg, 1)
            nc.scalar.activation(flog[:, 1, :], flog[:, 1, :], ACT.Exp).then_inc(z_exp, 1)
            act.wait_ge(z_neg, 2)
            nc.scalar.activation(lall[:], lall[:], ACT.Exp).then_inc(z_exp, 1)
            act.wait_ge(z_one, 1)
            nc.scalar.activation(flog[:, 1, :], flog[:, 1, :], ACT.Ln).then_inc(z_log, 1)
            act.wait_ge(z_one, 2)
            nc.scalar.activation(lall[:], lall[:], ACT.Ln).then_inc(z_log, 1)
            act.wait_ge(b_ready, 1)

            with act.Fori(0, BR.trips) as i:
                for q in range(BR.n):
                    round_panel(BR, i, q + LOOK)
                    if q == 0:
                        nc.scalar.activation(bh[:], ball[:, bass.ds(i, 1), :].rearrange("p a t -> p (a t)"),
                                             ACT.Copy, scale=1.0 / 16).then_inc(bh_ready, 1)
                        act.wait_ge(bh_ready, i + 1)
                        nc.scalar.activation(eb[:], bh[:], ACT.Exp).then_inc(eb_ready, 1)
                    if q == 3:
                        act.wait_ge(tri_sub, i + 1)
                        nc.scalar.activation(tri[:], tri[:], ACT.Exp).then_inc(tri_exp, 1)
                    if q == 4:
                        act.wait_ge(off_sub, i + 1)
                        nc.scalar.activation(kd[:], kd[:], ACT.Exp, scale=-1.0)
                        for u in range(1, 8):
                            keys = kh[:, :, u - 1, 0:SB * u]
                            nc.scalar.activation(keys, keys, ACT.Exp, scale=-1.0)
                        nc.scalar.activation(qh[:], qh[:], ACT.Exp).then_inc(off_exp, 1)
                    if q == 8:
                        act.wait_ge(kd_ps, i + 1)
                        nc.scalar.copy(kdtok0[:], AUX[0][0:META, 0:P])
                        nc.scalar.copy(kdtok[:], AUX[0][:, P:2 * P]).then_inc(kdtok_ready, 1)
                    if q == 10:
                        act.wait_ge(gv_ps, i + 1)
                        nc.scalar.copy(gvt[:].rearrange("p c v -> p (c v)"), AUX[2][:, 0:2 * DV])
                        nc.scalar.copy(gvt0[:], AUX[3][0:META, 0:DV]).then_inc(gvt_ready, 1)
                    if q == 12:
                        act.wait_ge(st0_ps, i + 1)
                        nc.scalar.copy(state[:, 0, :], AUX[3][:, 0:DV]).then_inc(st0_ready, 1)
                    if q == 15:
                        act.wait_ge(go_ps, i + 1)
                        nc.scalar.activation(osq[:], ps[:, 5:8:2, Q0:T], ACT.Square)
                        for e in range(2):
                            ins = nc.scalar.activation(on[:, e, :], AUX[1 + 2 * e][:, Q0:T], ACT.Copy,
                                                       scale=par[:, bass.ds(i * 2 + (GN + e), 1)])
                        ins.then_inc(go_copied, 1)
                    if q == 17:
                        act.wait_ge(vt_ps, i + 1)
                        nc.scalar.copy(vtok[:].rearrange("p c h d -> p (c h d)"), AUX[2])
                        nc.scalar.copy(vtok0[:].rearrange("p h d -> p (h d)"), AUX[1][0:META, 0:2 * P]).then_inc(vtok_ready, 1)
                    if q == 18:
                        act.wait_ge(gstat_inv, i + 1)
                        nc.scalar.activation(rstd[:, 0:NQ], rinv[:, 0:NQ], ACT.Sqrt).then_inc(gstat_root, 1)
                    if q == 21:
                        act.wait_ge(ctok_ps, i + 1)
                        nc.scalar.copy(ctok[:].rearrange("p b h -> p (b h)"), AUX[2][:, 0:2 * FH])
                        nc.scalar.copy(ctok0[:], AUX[2][0:META, 2 * FH:3 * FH]).then_inc(ctok_copied, 1)
                    if q in (22, 23):
                        h = q - 22
                        act.wait_ge(smax_ready, i * 2 + (h + 1))
                        for rows, a, b, t in ((P, 0, T, 0), (P, T, T + META + P, 1), (META, T + META + P, 432, 2)):
                            ins = nc.scalar.activation(sc[0:rows, h, a:b], sc[0:rows, h, a:b], ACT.Exp,
                                                       bias=nmax[0:rows, h, t:t + 1], accum_out=psum_row[0:rows, h, t:t + 1])
                        ins.then_inc(p_exp, 1)
                    if q == 25:
                        act.wait_ge(r_neg, i + 1)
                        nc.scalar.activation(sil[:], sil[:], ACT.Exp).then_inc(r_exp, 1)
                    if q in (26, 28):
                        h = (q - 26) // 2
                        act.wait_ge(pt_ps, i * 2 + (h + 1))
                        if h:
                            act.wait_ge(pv_ps, i * 2 + 1)
                        nc.scalar.copy(pt[:], AUX[0][:, 0:384])
                        nc.scalar.copy(pt0[:], AUX[2][0:META, 0:T]).then_inc(pt_copied, 1)
                    if q == 27:
                        act.wait_ge(oc_full, i + 1)
                        nc.scalar.copy(bo_h[:, 2, bass.ds(i * 2, 2), :], sil[:]).then_inc(oc_hi, 1)
                    if q == 30:
                        act.wait_ge(pv_ps, i * 2 + 2)
                        nc.scalar.copy(bo_h[:, 0, bass.ds(i * 2, 2), :], ps[:, 5:8:2, Q0:T]).then_inc(oa_hi, 1)
                    if q % 4 == 3:
                        pair = q // 4
                        st = pair % 2
                        pair_done(BR, i, q)
                        if pair == 0:
                            nc.scalar.mul(gqk[:, 0, :], ps[:, 0, 0:T], float(P) ** -0.5)
                            ins = nc.scalar.copy(gqk[:, 1, :], ps[:, 1, 0:T])
                        elif pair == 4:
                            ins = nc.scalar.mul(fq[:], pset(st, T), float(P) ** -0.5)
                        else:
                            dst, n = {1: (gv[:], T), 2: (fv[:], T), 3: (fk[:], T), 5: (gr, NQ), 6: (cc, NC), 7: (ch, NC), 8: (cb, NQ)}[pair]
                            ins = nc.scalar.copy(dst, pset(st, n))
                        ins.then_inc(set_free[st], 1)
                    if q == BR.n - 1:
                        act.wait_ge(ob_full, i + 1)
                        nc.scalar.copy(bo_h[:, 1, bass.ds(i * 2, 2), :], cy).then_inc(ob_hi, 1)

            with act.Fori(0, GT.trips) as i:
                for q in range(GT.n):
                    round_panel(GT, i, q + LOOK)
                    if q in (3, 7, 11):
                        g = q // 4
                        pair_done(GT, i, q)
                        for n in range(2):
                            ins = nc.scalar.activation(gate[:, g, n, :], ps[:, 2 * (g % 2) + n, 0:NQ], ACT.Sigmoid,
                                                       bias=par[:, bass.ds(i * 2 + (GB + g * KT + n), 1)])
                        ins.then_inc(set_free[g % 2], 1)
                    if q == GT.n - 1:
                        act.wait_ge(mix_full, i + 1)
                        nc.scalar.copy(mix_h[:, bass.ds(i * 2, 2), :], mixf[:]).then_inc(mix_hi, 1)

            with act.Fori(0, WO.trips) as i:
                for q in range(WO.n):
                    round_panel(WO, i, q + LOOK)
                    if q % 4 == 3:
                        pair = q // 4
                        act.wait_ge(set_free[pair], i + (WO_SET[pair] + 1))
                        nc.scalar.activation(osqm[:], hT[:, bass.ds(i * 4 + 2 * pair, 2), Q0:T], ACT.Square).then_inc(h2_squared, 1)
                        for n in range(2):
                            ins = nc.scalar.activation(xh[:, bass.ds(i * 4 + (2 * pair + n), 1), 0:NQ].rearrange("p a t -> p (a t)"),
                                                       hT[:, bass.ds(i * 4 + (2 * pair + n), 1), Q0:T].rearrange("p a t -> p (a t)"),
                                                       ACT.Copy, scale=par[:, bass.ds(i * 4 + (N2 + 2 * pair + n), 1)])
                        ins.then_inc(h2_hi, 1)

            def up_trip(i, first):
                for q in range(UP.n):
                    round_panel(UP, i, q + LOOK)
                    if first and q == 1:
                        act.wait_ge(r2_inv, 1)
                        nc.scalar.activation(rstd[:, 0:NQ], rinv[:, 0:NQ], ACT.Sqrt).then_inc(r2_root, 1)
                    if q == 5:
                        act.wait_ge(gate_conv, i + 1)
                        nc.scalar.activation(yg[:], yg[:], ACT.Silu).then_inc(gate_silu, 1)
                    if q == UP.n - 1:
                        act.wait_ge(act_full, i + 1)
                        nc.scalar.copy(act_h[:, bass.ds(i * 2, 2), :], yu[:]).then_inc(act_hi, 1)

            up_trip(0, True)
            with act.Fori(1, UP.trips) as i:
                up_trip(i, False)

            def down_trip(i, last):
                for q in range(DN.n):
                    if not (last and q + LOOK >= DN.n):
                        round_panel(DN, i, q + LOOK)
                    if q % 11 == 10:
                        pair = q // 11
                        act.wait_ge(set_free[pair], i + (DN_SET[pair] + 1))
                        nc.scalar.activation(sq3[:], h3[:], ACT.Square).then_inc(h3_squared, 1)
                        for n in range(2):
                            ins = nc.scalar.activation(hg[:, n, :], h3[:, n, :], ACT.Copy,
                                                       scale=par[:, bass.ds(i * 4 + (NF + 2 * pair + n), 1)])
                        ins.then_inc(h3_scaled, 1)

            with act.Fori(0, DN.trips - 1) as i:
                down_trip(i, False)
            down_trip(DN.trips - 1, True)
            act.wait_ge(fst_inv, 1)
            nc.scalar.activation(tokst[:, 2, :], tokst[:, 1, :], ACT.Sqrt).then_inc(fst_root, 1)

        @block.vector
        def _(dve):
            chain = [0, 0, 0]

            def link(ins):
                chain[2] += 1
                ins.then_inc(vec, 1)

            def linked(i):
                dve.wait_ge(vec, i * chain[1] + (chain[0] + chain[2]))

            def trip(per):
                chain[1], chain[2] = per, 0

            def trips_done(trips):
                assert chain[1] == chain[2], chain
                chain[0] += trips * chain[1]
                chain[1] = chain[2] = 0

            def straight_done():
                chain[0] += chain[2]
                chain[2] = 0

            def split_panel(ph, i, q):
                s = ph.slot(q)
                dve.wait_ge(hi_ready, ph.panel(i, q) + 1)
                nc.vector.tensor_tensor(lo[:, s, :], raw[:, s, :], hi[:, s, :].bitcast(F32),
                                        ALU.subtract).then_inc(lo_ready, 1)

            def pair_done(ph, i, q):
                dve.wait_ge(panel_used, ph.panel(i, q) + 1)

            def root_step(i, n):
                link(nc.vector.tensor_tensor(newt[:, 0:n], rstd[:, 0:n], rstd[:, 0:n], ALU.mult))
                linked(i)
                link(nc.vector.scalar_tensor_tensor(out=newt[:, 0:n], in0=newt[:, 0:n], scalar=-0.5, in1=var[:, 0:n],
                                                    op0=ALU.mult, op1=ALU.mult))
                linked(i)
                link(nc.vector.scalar_tensor_tensor(out=rstd[:, 0:n], in0=newt[:, 0:n], scalar=1.5, in1=rstd[:, 0:n],
                                                    op0=ALU.add, op1=ALU.mult))
                linked(i)

            trip(0)
            for kt in range(KT):
                dve.wait_ge(xt_ps, kt + 1)
                nc.vector.tensor_copy(hT[:, kt, :], AUX[kt % 4][:, 0:T]).then_inc(xt_copied, 1)
            for q in range(4):
                split_panel(PRO, 0, q)
            dve.wait_ge(stat_ps, 1)
            link(nc.vector.tensor_scalar(var[:], ps[:, 0, 0:T], 1.0 / D, EPS, ALU.mult, ALU.add))
            linked(0)
            nc.vector.reciprocal(rinv[:], var[:]).then_inc(stat_inv, 1)
            dve.wait_ge(stat_root, 1)
            root_step(0, T)
            dve.wait_ge(par_ok, 3)
            dve.wait_ge(xt_copied, KT)
            for kt in range(KT + 1):
                if kt < KT:
                    if kt >= 2:
                        dve.wait_ge(xn_lo, kt - 1)
                    nc.vector.scalar_tensor_tensor(out=xf[:, kt % 2, :], in0=hT[:, kt, :], scalar=par[:, N1 + kt:N1 + kt + 1],
                                                   in1=rstd[:], op0=ALU.mult, op1=ALU.mult).then_inc(xn_full, 1)
                if kt:
                    dve.wait_ge(xn_hi, kt)
                    nc.vector.tensor_tensor(xl[:, kt - 1, :], xf[:, (kt - 1) % 2, :], xh[:, kt - 1, :].bitcast(F32),
                                            ALU.subtract).then_inc(xn_lo, 1)
            nc.vector.memset(onesT[:], 1.0)
            nc.vector.memset(psum_row[:], 1.0)
            link(nc.vector.memset(every[:], 0.0))
            linked(0)
            link(nc.vector.memset(subs(every[:])[:, :, 0:1], 1.0))
            for q in range(LOOK):
                split_panel(BR, 0, q)
            dve.wait_ge(panel_used, 4)
            dve.wait_ge(small_in, 32)
            dve.wait_ge(glr_copied, 1)
            nc.vector.tensor_scalar(flog[:, 0, :], ps[0:FH, 0, 0:T], bf[:, 0:1], None, ALU.add).then_inc(set_free[0], 1)
            dve.wait_ge(set_free[0], 1)
            nc.vector.scalar_tensor_tensor(out=flog[:, 1, :], in0=flog[:, 0, :], scalar=-1.0, in1=flog[:, 0, :],
                                           op0=ALU.mult, op1=ALU.min).then_inc(z_neg, 1)
            dve.wait_ge(z_ps, 1)
            for g in range(GH):
                src = ps[:, 2 + g, 0:T]
                ins = nc.vector.tensor_scalar(zall[:, g, :], src, par[:, BG + g:BG + g + 1], None, ALU.add)
            ins.then_inc(set_free[1], 1)
            dve.wait_ge(set_free[1], 1)
            nc.vector.scalar_tensor_tensor(out=lall[:], in0=zall[:], scalar=-1.0, in1=zall[:],
                                           op0=ALU.mult, op1=ALU.min).then_inc(z_neg, 1)
            dve.wait_ge(z_exp, 1)
            nc.vector.tensor_scalar(flog[:, 1, :], flog[:, 1, :], 1.0, None, ALU.add).then_inc(z_one, 1)
            dve.wait_ge(z_exp, 2)
            nc.vector.tensor_scalar(lall[:], lall[:], 1.0, None, ALU.add).then_inc(z_one, 1)
            dve.wait_ge(z_log, 1)
            link(nc.vector.scalar_tensor_tensor(out=flog[:, 2, :], in0=flog[:, 0, :], scalar=0.0, in1=flog[:, 1, :],
                                                op0=ALU.min, op1=ALU.subtract))
            linked(0)
            nc.vector.tensor_tensor_scan(crow[:], onesT[0:FH, :], flog[:, 2, :], 0.0, ALU.mult, ALU.add).then_inc(c_ready, 1)
            dve.wait_ge(z_log, 2)
            link(nc.vector.scalar_tensor_tensor(out=zall[:], in0=zall[:], scalar=0.0, in1=lall[:],
                                                op0=ALU.min, op1=ALU.subtract))
            linked(0)
            for g in range(GH):
                for a, b in ((0, META), (META, META + P), (META + P, T)):
                    ins = nc.vector.tensor_tensor_scan(ball[:, g, a:b], onesT[:, a:b], zall[:, g, a:b], 0.0, ALU.mult, ALU.add)
            ins.then_inc(b_ready, 1)
            dve.wait_ge(c_ready, 1)
            dve.wait_ge(const_set, 9)
            dve.wait_ge(b_ready, 1)
            link(nc.vector.memset(kh[:], 0.0))
            linked(0)
            straight_done()

            with dve.Fori(0, BR.trips) as i:
                trip(18)
                for q in range(BR.n):
                    split_panel(BR, i, q + LOOK)
                    bs, q16, k16 = subs(bh[:]), subs(gqk[:, 0, :]), subs(gqk[:, 1, :])
                    if q == 0:
                        for h in range(2):
                            nc.vector.tensor_scalar(cneg[:, h, :], crow[:], ident[0:FH, bass.ds(i * 2 + h, 1)], -1.0,
                                                    ALU.mult, ALU.mult).then_inc(cneg_ready, 1)
                        dve.wait_ge(bh_ready, i + 1)
                    if q < 3:
                        for r in ((0, 1, 2, 3), (4, 5, 6, 7, 8), tuple(range(9, SB)))[q]:
                            ins = nc.vector.tensor_tensor(tri_r(r), bs[:, :, r:SB], bs[:, :, r:r + 1].broadcast_to([P, NSB, SB - r]),
                                                          ALU.subtract)
                        if q == 2:
                            ins.then_inc(tri_sub, 1)
                    if q == 3:
                        bc, bcs = chunks(bh[:]), chunk_subs(bh[:])
                        for u in range(1, 8):
                            nc.vector.tensor_tensor(kh[:, :, u - 1, 0:SB * u], bc[:, :, 0:SB * u],
                                                    bc[:, :, SB * u - 1:SB * u].broadcast_to([P, 2, SB * u]), ALU.subtract)
                        nc.vector.tensor_scalar(kd[:, 0:META], bh[:, 0:META], bh[:, META - 1:META], None, ALU.subtract)
                        nc.vector.tensor_scalar(kd[:, META:META + P], bh[:, META:META + P], bh[:, META + P - 1:META + P], None, ALU.subtract)
                        for c in range(2):
                            ins = nc.vector.tensor_tensor(qh[:, c], bcs[:, c, 1:8, :], bcs[:, c, 0:7, SB - 1:SB].broadcast_to([P, 7, SB]),
                                                          ALU.subtract)
                        ins.then_inc(off_sub, 1)
                    if q == 5:
                        dve.wait_ge(set_free[0], i * BR_PER[0] + (BR_SET[0] + 1))
                        dve.wait_ge(off_exp, i + 1)
                        nc.vector.tensor_tensor(kd[:], kd[:], gqk[:, 1, 0:META + P], ALU.mult).then_inc(kd_ready, 1)
                        kc = chunks(gqk[:, 1, :])
                        for u in range(1, 8):
                            nc.vector.tensor_tensor(kh[:, :, u - 1, 0:SB * u], kh[:, :, u - 1, 0:SB * u], kc[:, :, 0:SB * u], ALU.mult)
                        qcs = chunk_subs(gqk[:, 0, :])
                        for c in range(2):
                            ins = nc.vector.tensor_tensor(qh[:, c], qh[:, c], qcs[:, c, 1:8, :], ALU.mult)
                        ins.then_inc(off_ready, 1)
                        dve.wait_ge(eb_ready, i + 1)
                        nc.vector.tensor_tensor(qe[:], gqk[:, 0, :], eb[:], ALU.mult).then_inc(qe_ready, 1)
                    if q in (6, 7, 8):
                        if q == 6:
                            dve.wait_ge(tri_exp, i + 1)
                        for r in ((0, 1, 2, 3), (4, 5, 6, 7, 8), tuple(range(9, SB)))[q - 6]:
                            ins = nc.vector.tensor_tensor(tri_r(r), tri_r(r), k16[:, :, r:r + 1].broadcast_to([P, NSB, SB - r]), ALU.mult)
                        if q == 8:
                            link(ins)
                    if q in (9, 10, 11):
                        if q == 9:
                            linked(i)
                        for r in ((0, 1, 2, 3), (4, 5, 6, 7, 8), tuple(range(9, SB)))[q - 9]:
                            ins = nc.vector.tensor_tensor(tri_r(r), tri_r(r), q16[:, :, r:SB], ALU.mult)
                        if q == 11:
                            ins.then_inc(tri_ready, 1)
                    if q == 13:
                        dve.wait_ge(tri_ps, i + 1)
                        link(nc.vector.tensor_tensor(att[:], AUX[0][:, 0:T], blockd[:], ALU.mult))
                        dve.wait_ge(st0_ready, i + 1)
                        dve.wait_ge(st1_ps, i + 1)
                        nc.vector.scalar_tensor_tensor(out=state[:, 1, :], in0=state[:, 0, :], scalar=eb[:, META + P - 1:META + P],
                                                       in1=AUX[2][:, 0:DV], op0=ALU.mult, op1=ALU.add).then_inc(st1_ready, 1)
                        dve.wait_ge(off_ps, i + 1)
                        linked(i)
                        nc.vector.tensor_tensor(chunks(att[:])[:, :, SB:P], chunks(att[:])[:, :, SB:P],
                                                AUX[1][:, 0:2 * P].rearrange("p (c t) -> p c t", c=2)[:, :, SB:P],
                                                ALU.add).then_inc(att_ready, 1)
                    if q == 17:
                        dve.wait_ge(gstat_ps, i + 1)
                        link(nc.vector.tensor_scalar(var[:, 0:NQ], AUX[0][:, 0:NQ], 1.0 / DV, EPS, ALU.mult, ALU.add))
                        linked(i)
                        nc.vector.reciprocal(rinv[:, 0:NQ], var[:, 0:NQ]).then_inc(gstat_inv, 1)
                    if q == 19:
                        dve.wait_ge(gstat_root, i + 1)
                        root_step(i, NQ)
                        dve.wait_ge(go_copied, i + 1)
                        link(nc.vector.tensor_tensor(on, on, rstd[:, 0:NQ].unsqueeze(1).broadcast_to([P, 2, NQ]), ALU.mult))
                    if q in (21, 22):
                        h = q - 21
                        S = AUX[1 + 2 * h]
                        dve.wait_ge(score_ps, i * 2 + (h + 1))
                        dve.wait_ge(ctok_copied, i + 1)
                        c1, c2 = ctok[:, 0, bass.ds(i * 2 + h, 1)], ctok[:, 1, bass.ds(i * 2 + h, 1)]
                        nc.vector.scalar_tensor_tensor(out=sc[:, h, META + P:T], in0=S[:, META + P:T], scalar=c2, in1=causal[:],
                                                       op0=ALU.add, op1=ALU.add)
                        nc.vector.tensor_scalar(sc[:, h, 0:META + P], S[:, 0:META + P], c2, None, ALU.add)
                        nc.vector.scalar_tensor_tensor(out=sc[:, h, T + META:T + META + P], in0=S[:, T + META:T + META + P], scalar=c1,
                                                       in1=causal[:], op0=ALU.add, op1=ALU.add)
                        nc.vector.tensor_scalar(sc[:, h, T:T + META], S[:, T:T + META], c1, None, ALU.add)
                        link(nc.vector.scalar_tensor_tensor(out=sc[0:META, h, T + META + P:432], in0=S[0:META, T + META + P:432],
                                                            scalar=ctok0[:, bass.ds(i * 2 + h, 1)], in1=causal[0:META, 0:META],
                                                            op0=ALU.add, op1=ALU.add))
                        linked(i)
                        for rows, a, b, t in ((P, 0, T, 0), (P, T, T + META + P, 1), (META, T + META + P, 432, 2)):
                            ins = nc.vector.tensor_reduce(nmax[0:rows, h, t:t + 1], sc[0:rows, h, a:b], AX_X, ALU.max, negate=True)
                        ins.then_inc(smax_ready, 1)
                    if q == 24:
                        for h in range(2):
                            dve.wait_ge(p_exp, i * 2 + (h + 1))
                            link(nc.vector.reciprocal(pinv[:, h, :], psum_row[:, h, :]))
                            linked(i)
                            for rows, a, b, t in ((P, 0, T, 0), (P, T, T + META + P, 1), (META, T + META + P, 432, 2)):
                                ins = nc.vector.tensor_scalar(sc[0:rows, h, a:b], sc[0:rows, h, a:b], pinv[0:rows, h, t:t + 1],
                                                              None, ALU.mult)
                            ins.then_inc(p_ready, 1)
                        dve.wait_ge(set_free[1], i * BR_PER[1] + (BR_SET[1] + 3))
                        nc.vector.tensor_scalar(sil[:], gr, -1.0, 80.0, ALU.mult, ALU.min).then_inc(r_neg, 1)
                    if q == 26:
                        dve.wait_ge(r_exp, i + 1)
                        link(nc.vector.tensor_scalar(sil[:], sil[:], 1.0, None, ALU.add))
                        linked(i)
                        link(nc.vector.reciprocal(sil[:], sil[:]))
                        link(nc.vector.tensor_tensor(on, on, gr, ALU.mult))
                        linked(i)
                        nc.vector.tensor_tensor(sil[:], sil[:], on, ALU.mult).then_inc(oc_full, 1)
                    if q == 28:
                        dve.wait_ge(oc_hi, i + 1)
                        nc.vector.tensor_tensor(bo_l[:, 2, bass.ds(i * 2, 2), :], sil[:],
                                                bo_h[:, 2, bass.ds(i * 2, 2), :].bitcast(F32), ALU.subtract)
                    if q == 30:
                        dve.wait_ge(oa_hi, i + 1)
                        nc.vector.tensor_tensor(bo_l[:, 0, bass.ds(i * 2, 2), :], ps[:, 5:8:2, Q0:T],
                                                bo_h[:, 0, bass.ds(i * 2, 2), :].bitcast(F32), ALU.subtract)
                    if q == 32:
                        dve.wait_ge(set_free[1], i * BR_PER[1] + (BR_SET[1] + 4))
                        dve.wait_ge(set_free[0], i * BR_PER[0] + (BR_SET[0] + 4))
                        link(nc.vector.tensor_tensor(cc, cc, ch, ALU.mult))
                    if q == 33:
                        linked(i)
                        for k in range(CONV_K):
                            for n in range(2):
                                tap = cvw[:, k, bass.ds(i * 2 + n, 1)]
                                if k == 0:
                                    ins = nc.vector.tensor_scalar(cy[:, n, :], cc[:, n, 0:NQ], tap, None, ALU.mult)
                                else:
                                    ins = nc.vector.scalar_tensor_tensor(out=cy[:, n, :], in0=cc[:, n, k:k + NQ], scalar=tap,
                                                                         in1=cy[:, n, :], op0=ALU.mult, op1=ALU.add)
                            link(ins)
                            linked(i)
                    if q == BR.n - 1:
                        dve.wait_ge(set_free[0], i * BR_PER[0] + (BR_SET[0] + 5))
                        nc.vector.tensor_tensor(cy, cy, cb, ALU.mult).then_inc(ob_full, 1)
                        dve.wait_ge(ob_hi, i + 1)
                        nc.vector.tensor_tensor(bo_l[:, 1, bass.ds(i * 2, 2), :], cy,
                                                bo_h[:, 1, bass.ds(i * 2, 2), :].bitcast(F32), ALU.subtract).then_inc(bo_lo, 1)
                trips_done(BR.trips)

            with dve.Fori(0, GT.trips) as i:
                trip(1)
                for q in range(GT.n):
                    split_panel(GT, i, q + LOOK)
                    if q == 13:
                        dve.wait_ge(set_free[0], i * 3 + (GT_SET[0] + 1))
                        pair_done(GT, i, q)
                        nc.vector.tensor_tensor(mixf[:], pset(1, NQ), gate[:, 0], ALU.mult).then_inc(set_free[1], 1)
                    if q == 15:
                        dve.wait_ge(set_free[1], i * 3 + (GT_SET[1] + 2))
                        pair_done(GT, i, q)
                        nc.vector.tensor_tensor(mixt[:], pset(0, NQ), gate[:, 1], ALU.mult).then_inc(set_free[0], 1)
                        dve.wait_ge(set_free[0], i * 3 + (GT_SET[0] + 3))
                        link(nc.vector.tensor_tensor(mixf[:], mixf[:], mixt[:], ALU.add))
                        linked(i)
                    if q == 17:
                        pair_done(GT, i, q)
                        nc.vector.tensor_tensor(mixt[:], pset(1, NQ), gate[:, 2], ALU.mult).then_inc(set_free[1], 1)
                        dve.wait_ge(set_free[1], i * 3 + (GT_SET[1] + 3))
                        nc.vector.tensor_tensor(mixf[:], mixf[:], mixt[:], ALU.add).then_inc(mix_full, 1)
                        dve.wait_ge(mix_hi, i + 1)
                        nc.vector.tensor_tensor(mix_l[:, bass.ds(i * 2, 2), :], mixf[:],
                                                mix_h[:, bass.ds(i * 2, 2), :].bitcast(F32), ALU.subtract).then_inc(mix_lo, 1)
                trips_done(GT.trips)

            link(nc.vector.memset(sqsum[:], 0.0))
            linked(0)
            straight_done()
            with dve.Fori(0, WO.trips) as i:
                for q in range(WO.n):
                    split_panel(WO, i, q + LOOK)
                    if q % 4 == 3:
                        pair = q // 4
                        at = bass.ds(i * 4 + 2 * pair, 2)
                        pair_done(WO, i, q)
                        nc.vector.tensor_tensor(hT[:, at, Q0:T], hT[:, at, Q0:T], pset(pair, NQ), ALU.add).then_inc(set_free[pair], 1)
                        dve.wait_ge(h2_squared, i * 2 + (pair + 1))
                        for n in range(2):
                            nc.vector.tensor_tensor(sqsum[:, 0:NQ], sqsum[:, 0:NQ], osqm[:, n, :], ALU.add).then_inc(h2sq_sum, 1)
                            dve.wait_ge(h2sq_sum, i * 4 + (2 * pair + n + 1))
                        dve.wait_ge(h2_hi, i * 2 + (pair + 1))
                        for n in range(2):
                            one = bass.ds(i * 4 + (2 * pair + n), 1)
                            ins = nc.vector.scalar_tensor_tensor(
                                out=xl[:, one, 0:NQ], in0=hT[:, one, Q0:T], scalar=par[:, bass.ds(i * 4 + (N2 + 2 * pair + n), 1)],
                                in1=xh[:, one, 0:NQ].bitcast(F32), op0=ALU.mult, op1=ALU.subtract)
                        ins.then_inc(h2_lo, 1)

            def up_trip(i, first):
                trip(5)
                for q in range(UP.n):
                    split_panel(UP, i, q + LOOK)
                    if first and q == 0:
                        dve.wait_ge(r2_ps, 1)
                        nc.vector.tensor_scalar(var[:, 0:NQ], AUX[0][:, 0:NQ], 1.0 / D, EPS, ALU.mult, ALU.add).then_inc(r2_step, 1)
                        dve.wait_ge(r2_step, 1)
                        nc.vector.reciprocal(rinv[:, 0:NQ], var[:, 0:NQ]).then_inc(r2_inv, 1)
                    if first and q == 2:
                        dve.wait_ge(r2_root, 1)
                        nc.vector.tensor_tensor(newt[:, 0:NQ], rstd[:, 0:NQ], rstd[:, 0:NQ], ALU.mult).then_inc(r2_step, 1)
                        dve.wait_ge(r2_step, 2)
                        nc.vector.scalar_tensor_tensor(out=newt[:, 0:NQ], in0=newt[:, 0:NQ], scalar=-0.5, in1=var[:, 0:NQ],
                                                       op0=ALU.mult, op1=ALU.mult).then_inc(r2_step, 1)
                        dve.wait_ge(r2_step, 3)
                        nc.vector.scalar_tensor_tensor(out=rstd[:, 0:NQ], in0=newt[:, 0:NQ], scalar=1.5, in1=rstd[:, 0:NQ],
                                                       op0=ALU.add, op1=ALU.mult).then_inc(r2_step, 1)
                        dve.wait_ge(r2_step, 4)
                    if q % 4 == 3:
                        half = q // 4
                        y = yu if half else yg
                        pair_done(UP, i, q)
                        nc.vector.tensor_tensor(uu[:], pset(half, NQ), rstd[:, 0:NQ].unsqueeze(1).broadcast_to([P, 2, NQ]),
                                                ALU.mult).then_inc(set_free[half], 1)
                        dve.wait_ge(set_free[half], i + (UP_SET[half] + 1))
                        for k in range(CONV_K):
                            for n in range(2):
                                tap = mcw[:, k, bass.ds(i * 2 + (half * FT + n), 1)]
                                if k == 0:
                                    ins = nc.vector.tensor_scalar(y[:, n, :], uu[:, n, 0:SEQ], tap, None, ALU.mult)
                                else:
                                    ins = nc.vector.scalar_tensor_tensor(out=y[:, n, :], in0=uu[:, n, k:k + SEQ], scalar=tap,
                                                                         in1=y[:, n, :], op0=ALU.mult, op1=ALU.add)
                            if k == CONV_K - 1 and not half:
                                ins.then_inc(gate_conv, 1)
                            else:
                                link(ins)
                                linked(i)
                    if q == UP.n - 1:
                        dve.wait_ge(gate_silu, i + 1)
                        nc.vector.tensor_tensor(yu[:], yu[:], yg[:], ALU.mult).then_inc(act_full, 1)
                        dve.wait_ge(act_hi, i + 1)
                        nc.vector.tensor_tensor(act_l[:, bass.ds(i * 2, 2), :], yu[:],
                                                act_h[:, bass.ds(i * 2, 2), :].bitcast(F32), ALU.subtract).then_inc(act_lo, 1)

            up_trip(0, True)
            with dve.Fori(1, UP.trips) as i:
                up_trip(i, False)
            trips_done(UP.trips)

            link(nc.vector.memset(sqsum[:], 0.0))
            linked(0)
            straight_done()

            def copy_rows(pair, i, count):
                dve.wait_ge(yt_ps, count)
                nc.vector.tensor_copy(ybuf[:, :, bass.ds(i * (2 * COLS) + pair * COLS, COLS)],
                                      AUX[pair].rearrange("p (b n) -> p b n", b=2)).then_inc(yt_copied, 1)

            def down_trip(i, first, last):
                trip(4)
                for q in range(DN.n):
                    if not (last and q + LOOK >= DN.n):
                        split_panel(DN, i, q + LOOK)
                    if q == 4 and not first:
                        copy_rows(1, i - 1, i * 2)
                    if q == 15:
                        copy_rows(0, i, i * 2 + 1)
                    if q % 11 == 10:
                        pair = q // 11
                        pair_done(DN, i, q)
                        nc.vector.tensor_tensor(h3[:], hT[:, bass.ds(i * 4 + 2 * pair, 2), META:T], pset(pair, SEQ),
                                                ALU.add).then_inc(set_free[pair], 1)
                        dve.wait_ge(h3_squared, i * 2 + (pair + 1))
                        for n in range(2):
                            link(nc.vector.tensor_tensor(sqsum[:, 0:SEQ], sqsum[:, 0:SEQ], sq3[:, n, :], ALU.add))
                            linked(i)

            down_trip(0, True, False)
            with dve.Fori(1, DN.trips - 1) as i:
                down_trip(i, False, False)
            down_trip(DN.trips - 1, False, True)
            trips_done(DN.trips)
            link(nc.vector.memset(tokst[:], 0.0))
            nc.vector.tensor_copy(newt[:, 0:1], sqsum[:, 0:1]).then_inc(fst_sum, 1)
            dve.wait_ge(fst_ps, 1)
            linked(0)
            link(nc.vector.tensor_scalar(tokst[:, 0, :], AUX[2][:, 0:2], 1.0 / D, EPS, ALU.mult, ALU.add))
            linked(0)
            nc.vector.reciprocal(tokst[:, 1, :], tokst[:, 0, :]).then_inc(fst_inv, 1)
            copy_rows(1, DN.trips - 1, 2 * DN.trips)
            dve.wait_ge(fst_root, 1)
            link(nc.vector.tensor_tensor(tokst[:, 3, :], tokst[:, 2, :], tokst[:, 2, :], ALU.mult))
            linked(0)
            link(nc.vector.scalar_tensor_tensor(out=tokst[:, 3, :], in0=tokst[:, 3, :], scalar=-0.5, in1=tokst[:, 0, :],
                                                op0=ALU.mult, op1=ALU.mult))
            linked(0)
            link(nc.vector.scalar_tensor_tensor(out=tokst[:, 2, :], in0=tokst[:, 3, :], scalar=1.5, in1=tokst[:, 2, :],
                                                op0=ALU.add, op1=ALU.mult))
            linked(0)
            dve.wait_ge(yt_copied, 2 * DN.trips)
            for b in range(2):
                for h in range(2):
                    quarter = ybuf[:, b, h * (D // 2):(h + 1) * (D // 2)]
                    nc.vector.tensor_scalar(quarter, quarter, tokst[:, 2, b:b + 1], None, ALU.mult).then_inc(y_scaled, 1)

        @block.tensor
        def _(pe):
            def use_panel(ph, i, q, st, moving, n, first, last, kts=KJ):
                pe.wait_ge(lo_ready, ph.panel(i, q) + 1)
                s = ph.slot(q)
                for m in range(2):
                    acc = ps[:, 2 * st + m, 0:n]
                    for j in range(kts):
                        mh, ml = moving(j)
                        w_hi, w_lo = tiles(hi, s, j, m), tiles(lo, s, j, m)
                        nc.tensor.matmul(acc, w_hi, mh, start=first and j == 0, stop=False)
                        nc.tensor.matmul(acc, w_hi, ml, start=False, stop=False)
                        ins = nc.tensor.matmul(acc, w_lo, mh, start=False, stop=last and j == kts - 1)
                ins.then_inc(panel_used, 1)

            def x_window(kt0, a, n):
                return lambda j: (xh[:, kt0 + j, a:a + n], xl[:, kt0 + j, a:a + n])

            pe.wait_ge(const_set, 3)
            for b in range(3):
                pe.wait_ge(x_in[b], 16)
            for kt in range(KT):
                if kt >= 4:
                    pe.wait_ge(xt_copied, kt - 3)
                bank = AUX[kt % 4]
                cols = slice(kt * P, (kt + 1) * P)
                nc.tensor.transpose(bank[:, 0:META], xa[:, cols], ident[0:META, 0:META])
                for b in range(2):
                    ins = nc.tensor.transpose(bank[:, META + b * P:META + (b + 1) * P], xb[:, b, cols], ident[:])
                ins.then_inc(xt_ps, 1)
            pe.wait_ge(par_in, 160)
            nc.tensor.transpose(ps[:, 2, 0:NPAR], prow[0:NPAR, 0, :], ident[0:NPAR, 0:NPAR])
            nconv = CONV_K * CH // P
            nc.tensor.transpose(ps[:, 2, P:P + nconv], prow[0:nconv, 1, :], ident[0:nconv, 0:nconv])
            for k in range(CONV_K):
                ins = nc.tensor.transpose(ps[:, 3, k * 2 * FT:(k + 1) * 2 * FT], prow[0:2 * FT, 2 + k, :], ident[0:2 * FT, 0:2 * FT])
            ins.then_inc(par_t, 1)
            pe.wait_ge(xsq_sum, KT)
            nc.tensor.matmul(ps[:, 0, 0:T], ones[:], sqsum[:], start=True, stop=True).then_inc(stat_ps, 1)
            for q in range(4):
                pe.wait_ge(xn_lo, KJ * (q + 1))
                use_panel(PRO, 0, q, 0, x_window(q * KJ, 0, T), T, q == 0, q == 3)
            pe.wait_ge(glr_copied, 1)
            pe.wait_ge(small_in, 32)
            pe.wait_ge(par_ok, 3)
            for g in range(GH):
                ins = nc.tensor.matmul(ps[:, 2 + g, 0:T], wg2[:, g * P:(g + 1) * P], glr[:], start=True, stop=True)
            ins.then_inc(z_ps, 1)

            def gla_state_parts(i, q):
                if q == 7:
                    pe.wait_ge(kd_ready, i + 1)
                    nc.tensor.transpose(AUX[0][0:META, 0:P], kd[:, 0:META], ident[:])
                    nc.tensor.transpose(AUX[0][:, P:2 * P], kd[:, META:META + P], ident[:]).then_inc(kd_ps, 1)
                if q == 8:
                    pe.wait_ge(off_ready, i + 1)
                    for c in range(2):
                        for u in range(1, 8):
                            ins = nc.tensor.matmul(AUX[1][:, c * P + u * SB:c * P + (u + 1) * SB], kh[:, c, u - 1, :],
                                                   qh[:, c, u - 1, :], start=True, stop=True)
                    ins.then_inc(off_ps, 1)
                if q == 9:
                    pe.wait_ge(set_free[1], i * BR_PER[1] + (BR_SET[1] + 1))
                    for e in range(2):
                        for c in range(2):
                            nc.tensor.transpose(AUX[2][:, c * DV + e * P:c * DV + (e + 1) * P],
                                                gv[:, e, META + c * P:META + (c + 1) * P], ident[:])
                        ins = nc.tensor.transpose(AUX[3][0:META, e * P:(e + 1) * P], gv[:, e, 0:META], ident[:])
                    ins.then_inc(gv_ps, 1)
                if q == 11:
                    pe.wait_ge(kdtok_ready, i + 1)
                    pe.wait_ge(gvt_ready, i + 1)
                    nc.tensor.matmul(AUX[3][:, 0:DV], kdtok0[:], gvt0[:], start=True, stop=True).then_inc(st0_ps, 1)
                if q == 12:
                    pe.wait_ge(tri_ready, i + 1)
                    for r in range(SB):
                        ins = nc.tensor.matmul(subs(AUX[0][:, 0:T])[:, :, r:SB], every[:, SB - r:SB - r + P], tri_r(r),
                                               start=(r == 0), stop=(r == SB - 1))
                    ins.then_inc(tri_ps, 1)
                    nc.tensor.matmul(AUX[2][:, 0:DV], kdtok[:], gvt[:, 0, :], start=True, stop=True).then_inc(st1_ps, 1)

            def gla_output(i):
                pe.wait_ge(st1_ready, i + 1)
                pe.wait_ge(att_ready, i + 1)
                pe.wait_ge(qe_ready, i + 1)
                for e in range(2):
                    o = AUX[1 + 2 * e]
                    cols = slice(e * P, (e + 1) * P)
                    ins = nc.tensor.matmul(o[:, 0:META], gvt0[:, cols], att[0:META, 0:META], start=True, stop=True)
                    for c in range(2):
                        tok = slice(META + c * P, META + (c + 1) * P)
                        nc.tensor.matmul(o[:, tok], gvt[:, c, cols], att[:, tok], start=True, stop=False)
                        ins = nc.tensor.matmul(o[:, tok], state[:, c, cols], qe[:, tok], start=False, stop=True)
                ins.then_inc(go_ps, 1)

            def fox_scores(i):
                pe.wait_ge(set_free[0], i * BR_PER[0] + (BR_SET[0] + 3))
                pe.wait_ge(set_free[1], i * BR_PER[1] + (BR_SET[1] + 2))
                pe.wait_ge(cneg_ready, i * 2 + 2)
                pe.wait_ge(vtok_ready, i + 1)
                for h in range(2):
                    S = AUX[1 + 2 * h]
                    for rows, at, q_at, keys in ((P, 0, META + P, T), (P, T, META, META + P), (META, T + META + P, 0, META)):
                        nc.tensor.matmul(S[0:rows, at:at + keys], fq[:, h, q_at:q_at + rows], fk[:, h, 0:keys], start=True, stop=False)
                        ins = nc.tensor.matmul(S[0:rows, at:at + keys], ones[0:FH, 0:rows], cneg[:, h, 0:keys], start=False, stop=True)
                    ins.then_inc(score_ps, 1)
                for c in range(2):
                    nc.tensor.transpose(AUX[2][:, c * FH:(c + 1) * FH], crow[:, META + c * P:META + (c + 1) * P],
                                        ident[0:FH, 0:FH])
                nc.tensor.transpose(AUX[2][0:META, 2 * FH:3 * FH], crow[:, 0:META], ident[0:FH, 0:FH]).then_inc(ctok_ps, 1)

            def fox_transposes(i, h):
                pe.wait_ge(p_ready, i * 2 + (h + 1))
                if h == 0:
                    pe.wait_ge(ctok_copied, i + 1)
                else:
                    pe.wait_ge(pt_copied, i * 2 + 1)
                t1 = T
                nc.tensor.transpose(AUX[0][:, 0:P], sc[:, h, META + P:T], ident[:])
                nc.tensor.transpose(AUX[0][:, P:2 * P], sc[:, h, META:META + P], ident[:])
                nc.tensor.transpose(AUX[0][:, 2 * P:3 * P], sc[:, h, t1 + META:t1 + META + P], ident[:])
                nc.tensor.transpose(AUX[2][0:META, 0:P], sc[:, h, 0:META], ident[:])
                nc.tensor.transpose(AUX[2][0:META, P:2 * P], sc[:, h, t1:t1 + META], ident[:])
                nc.tensor.transpose(AUX[2][0:META, 2 * P:2 * P + META], sc[0:META, h, t1 + META + P:t1 + 2 * META + P],
                                    ident[0:META, 0:META]).then_inc(pt_ps, 1)

            def fox_output(i, h):
                pe.wait_ge(pt_copied, i * 2 + (h + 1))
                o = AUX[1 + 2 * h]
                nc.tensor.matmul(o[:, META + P:T], vtok[:, 1, h, :], pt[:, 0:P], start=True, stop=False)
                nc.tensor.matmul(o[:, META + P:T], vtok[:, 0, h, :], pt[:, P:2 * P], start=False, stop=False)
                nc.tensor.matmul(o[:, META + P:T], vtok0[:, h, :], pt0[:, 0:P], start=False, stop=True)
                nc.tensor.matmul(o[:, META:META + P], vtok[:, 0, h, :], pt[:, 2 * P:3 * P], start=True, stop=False)
                nc.tensor.matmul(o[:, META:META + P], vtok0[:, h, :], pt0[:, P:2 * P], start=False, stop=True)
                nc.tensor.matmul(o[:, 0:META], vtok0[:, h, :], pt0[:, 2 * P:2 * P + META], start=True, stop=True).then_inc(pv_ps, 1)

            window = [(0, T)] * 5 + [(Q0, NQ), (C0, NC), (C0, NC), (Q0, NQ)]
            with pe.Fori(0, BR.trips) as i:
                for q in range(BR.n):
                    pair = q // 4
                    st = pair % 2
                    if q % 4 == 0:
                        pe.wait_ge(set_free[st], i * BR_PER[st] + (BR_SET[st] + pair // 2))
                    a, n = window[pair]
                    use_panel(BR, i, q, st, x_window((q % 4) * KJ, a, n), n, q % 4 == 0, q % 4 == 3)
                    gla_state_parts(i, q)
                    if q == 14:
                        gla_output(i)
                    if q == 16:
                        pe.wait_ge(go_copied, i + 1)
                        for e in range(2):
                            ins = nc.tensor.matmul(AUX[0][:, 0:NQ], ones[:], osq[:, e, :], start=(e == 0), stop=(e == 1))
                        ins.then_inc(gstat_ps, 1)
                        pe.wait_ge(set_free[0], i * BR_PER[0] + (BR_SET[0] + 2))
                        for h in range(2):
                            for c in range(2):
                                nc.tensor.transpose(AUX[2][:, (2 * c + h) * P:(2 * c + h + 1) * P],
                                                    fv[:, h, META + c * P:META + (c + 1) * P], ident[:])
                            ins = nc.tensor.transpose(AUX[1][0:META, h * P:(h + 1) * P], fv[:, h, 0:META], ident[:])
                        ins.then_inc(vt_ps, 1)
                    if q == 20:
                        fox_scores(i)
                    if q == 25:
                        fox_transposes(i, 0)
                    if q == 27:
                        fox_transposes(i, 1)
                        fox_output(i, 0)
                    if q == 29:
                        fox_output(i, 1)

            with pe.Fori(0, GT.trips) as i:
                for q in range(GT.n):
                    if q < 12:
                        g, kq = q // 4, q % 4
                        st, before = g % 2, g // 2
                        mv = x_window(kq * KJ, Q0, NQ)
                        last = 3
                    else:
                        g, kq = (q - 12) // 2, q % 2
                        st, before = (g + 1) % 2, 1 + (g + 1) // 2
                        mv = (lambda g, k0: lambda j: (bo_h[:, g, k0 + j, :], bo_l[:, g, k0 + j, :]))(g, kq * KJ)
                        last = 1
                    if kq == 0:
                        pe.wait_ge(set_free[st], i * 3 + (GT_SET[st] + before))
                    if q == 12:
                        pe.wait_ge(bo_lo, BR.trips)
                    use_panel(GT, i, q, st, mv, NQ, kq == 0, kq == last)

            with pe.Fori(0, WO.trips) as i:
                for q in range(WO.n):
                    st, kq = q // 4, q % 4
                    if kq == 0:
                        pe.wait_ge(set_free[st], i + WO_SET[st])
                    pe.wait_ge(mix_lo, 2 * kq + 2)
                    use_panel(WO, i, q, st, (lambda k0: lambda j: (mix_h[:, k0 + j, :], mix_l[:, k0 + j, :]))(kq * KJ),
                              NQ, kq == 0, kq == 3)

            def up_trip(i, first):
                for q in range(UP.n):
                    st, kq = q // 4, q % 4
                    if kq == 0:
                        pe.wait_ge(set_free[st], i + UP_SET[st])
                    if first:
                        pe.wait_ge(h2_lo, 2 * kq + 2)
                    use_panel(UP, i, q, st, x_window(kq * KJ, 0, NQ), NQ, kq == 0, kq == 3)
                    if first and q == 0:
                        pe.wait_ge(h2sq_sum, KT)
                        nc.tensor.matmul(AUX[0][:, 0:NQ], ones[:], sqsum[:, 0:NQ], start=True, stop=True).then_inc(r2_ps, 1)

            up_trip(0, True)
            with pe.Fori(1, UP.trips) as i:
                up_trip(i, False)

            def transpose_rows(pair, count):
                pe.wait_ge(h3_scaled, count)
                if not isinstance(count, int) or count > 1:
                    pe.wait_ge(yt_copied, count - 1)
                for b in range(2):
                    for n in range(2):
                        ins = nc.tensor.transpose(AUX[pair][:, b * COLS + n * P:b * COLS + (n + 1) * P],
                                                  hg[:, n, b * P:(b + 1) * P], ident[:])
                ins.then_inc(yt_ps, 1)

            def down_trip(i, first):
                for q in range(DN.n):
                    st, kq = q // 11, q % 11
                    if kq == 0:
                        pe.wait_ge(set_free[st], i + DN_SET[st])
                    if first and st == 0:
                        pe.wait_ge(act_lo, 2 * kq + 2)
                    use_panel(DN, i, q, st, (lambda k0: lambda j: (act_h[:, k0 + j, :], act_l[:, k0 + j, :]))(kq * KJ),
                              SEQ, kq == 0, kq == 10)
                    if q == 2 and not first:
                        transpose_rows(1, i * 2)
                    if q == 13:
                        transpose_rows(0, i * 2 + 1)

            down_trip(0, True)
            with pe.Fori(1, DN.trips - 1) as i:
                down_trip(i, False)
            down_trip(DN.trips - 1, False)
            pe.wait_ge(fst_sum, 1)
            for b in range(2):
                ins = nc.tensor.matmul(AUX[2][:, b:b + 1], sqsum[:, b * P:(b + 1) * P], ones[:, 0:1], start=True, stop=True)
            ins.then_inc(fst_ps, 1)
            transpose_rows(1, 2 * DN.trips)


_INS = ['x', 'meta_tokens', 'norm1_g', 'w_in', 'fox_b_f', 'gate_b', 'conv_w', 'gla_w_g2', 'gla_b_g', 'gla_norm_g',
        'w_a_o', 'w_b_o', 'w_c_o', 'w_o', 'norm2_g', 'w_up', 'mlp_conv_w', 'w_down', 'final_norm_g']


def kernel(**inputs):
    import numpy as _np
    import concourse.bacc as _bacc
    from concourse import mybir as _mybir
    from concourse.bass_utils import run_bass_kernel_spmd as _run

    nc = _bacc.Bacc("TRN2", target_bir_lowering=False, num_devices=1)
    arrays, args = {}, []
    for name in _INS:
        a = _np.ascontiguousarray(inputs[name])
        arrays[f"in_{name}_dram"] = a
        args.append(nc.dram_tensor(f"in_{name}_dram", a.shape, _mybir.dt.from_np(a.dtype), kind="ExternalInput").ap())
    args.append(nc.dram_tensor("out_dram", inputs['x'].shape, F32, kind="ExternalOutput").ap())
    hybrid_layer(nc, *args)
    r = _run(nc, [arrays], core_ids=[0])
    return r.results[0]["out_dram"]
```

```python
from contextlib import ExitStack

import concourse.bass as bass
from concourse import mybir

ALU = mybir.AluOpType
ACT = mybir.ActivationFunctionType
F32 = mybir.dt.float32
F32R = mybir.dt.float32r
AX_X = mybir.AxisListType.X

P = 128
EPS = 1e-6
NEG = -1e30
SLOTS = 4
LOOK = 3
KJ = 4
COLS = 256
YP = 4


class Phase:

    def __init__(self, prev, trips, segments):
        self.trips, self.n = trips, sum(segments)
        self.base = prev.base + prev.trips * prev.n if prev else SLOTS
        self.land0 = [prev.land0[s] + prev.trips * prev.uses[s] for s in range(SLOTS)] if prev else [0] * SLOTS
        last = min(segments[-1], prev.segments[-1]) if prev else SLOTS
        self.segments = segments
        self.place = [(m, s) for m, length in enumerate(segments) for s in range(length)]
        self.back = [last if m == 0 else segments[m - 1] for m, _ in self.place]
        self.uses = [1 + sum(1 for length in segments if length > s) for s in range(SLOTS)]

    def wrap(self, i, q):
        return (i, q) if q < self.n else (i + 1, q - self.n)

    def slot(self, q):
        return self.place[q % self.n][1]

    def panel(self, i, q):
        return i * self.n + (self.base + q)

    def before(self, i, q):
        return self.panel(i, q) - self.back[q % self.n] + 1

    def landed(self, i, q):
        i, q = self.wrap(i, q)
        m, s = self.place[q]
        loads = 1 + sum(1 for length in self.segments[:m + 1] if length > s)
        return (i * self.uses[s]) * 16 + 16 * (self.land0[s] + loads)


def hybrid_layer(nc, x, meta_tokens, norm1_g, w_in, fox_b_f, gate_b, conv_w, gla_w_g2, gla_b_g,
                 gla_norm_g, w_a_o, w_b_o, w_c_o, w_o, norm2_g, w_up, mlp_conv_w, w_down,
                 final_norm_g, out):
    _, SEQ, D = x.shape
    META = meta_tokens.shape[0]
    T = META + SEQ
    KT = D // P
    FH = fox_b_f.shape[1]
    CONV_K, CH = conv_w.shape[1:]
    FW = w_a_o.shape[1]
    RANK, GK = gla_w_g2.shape[1:]
    GH = GK // P
    GV = w_c_o.shape[1]
    DFF = w_down.shape[1]
    FT = DFF // P
    BKT = FW // P
    Q0 = META - (CONV_K - 1)
    NQ = T - Q0
    QM = META - Q0
    C0 = Q0 - (CONV_K - 1)
    NC = T - C0
    SB = 8
    LEVELS = (64, 32, 16, 8)
    LV = len(LEVELS)
    NA, NB = 3 * P + META, 4 * P
    NSB = T // SB
    DV = GV // GH
    assert META == 2 * SB and SEQ == 2 * P and FW == CH == GV == 8 * P and DV == 2 * P and CONV_K == 3

    FOX_Q = 0
    FOX_K = FOX_Q + FW
    FOX_V = FOX_K + FW
    FOX_F = FOX_V + FW
    SC_B = FOX_F + FH
    SC_C = SC_B + CH
    SC_H = SC_C + CH
    GLA_Q = SC_H + CH
    GLA_K = GLA_Q + GK
    GLA_V = GLA_K + GK
    GLA_R = GLA_V + GV
    GLA_LR = GLA_R + GV
    GATES = GLA_LR + RANK
    SM_LR, SM_N = 32, 48

    BR = Phase(None, GH, [4] * 9)
    GT = Phase(BR, D // COLS, [4, 4, 4, 3, 3])
    WO = Phase(GT, D // COLS // 2, [4, 4])
    UP = Phase(WO, DFF // COLS, [4, 4])
    DN = Phase(UP, D // COLS // 2, [4, 4, 3, 4, 4, 3])
    BR_SET, BR_PER = (1, 1), (4, 4)
    GT_SET = tuple(BR_SET[s] + BR.trips * BR_PER[s] for s in range(2))
    WO_SET = tuple(GT_SET[s] + GT.trips * 3 for s in range(2))
    UP_SET = tuple(WO_SET[s] + WO.trips for s in range(2))
    DN_SET = tuple(UP_SET[s] + UP.trips for s in range(2))

    with ExitStack() as ctx:
        def sem(name):
            return ctx.enter_context(nc.semaphore(name))

        keep = ExitStack()

        def sb(name, shape, dt=F32, scope=None):
            return (scope or keep).enter_context(nc.sbuf_tensor(name, shape, dt))

        ps = ctx.enter_context(nc.psum_tensor("ps", [P, 8, 512], F32))
        AUX = [ps[:, 4 + b, :] for b in range(4)]

        def pset(s, n):
            return ps[:, 4:7:2, 0:n] if s == 2 else ps[:, 2 * s:2 * s + 2, 0:n]

        raw = sb("raw", [P, SLOTS, KJ * COLS])
        hi = sb("hi", [P, SLOTS, KJ * COLS], F32R)
        lo = sb("lo", [P, SLOTS, KJ * COLS], F32R)
        hT = sb("hT", [P, KT, T])
        par = sb("par", [P, 3 * KT + 3 * KT + 8 + GH])
        cvw = sb("cvw", [P, CONV_K, CH // P])
        mcw = sb("mcw", [P, CONV_K, 2 * FT])
        N2, NF, GB, GN, BG = KT, 2 * KT, 3 * KT, 6 * KT, 6 * KT + 8
        NPAR = BG + GH
        ones_r = sb("ones_r", [32 + FH, P], F32R)
        ident = sb("ident", [P, P])
        ones = sb("ones", [P, P])
        var = sb("var", [P, T])
        newt = sb("newt", [P, T])
        rinv = newt
        rstd = sb("rstd", [P, T])
        rs1 = sb("rs1", [P, T])
        sqsum = rs1
        g1 = sb("g1", [P, KT])
        warm = sb("warm", [P, 1])
        tokst = sb("tokst", [P, 4, 2])
        bf = sb("bf", [FH, 1])

        xn_scope = ExitStack()
        xh = sb("xh", [P, KT, T], F32R, xn_scope)
        xl = sb("xl", [P, KT, T], F32R, xn_scope)

        narrow = ExitStack()
        nw = sb("nw", [P, KT * SM_N + P - SM_N], F32, narrow)
        nw_h = sb("nw_h", [P, KT * SM_N + P - SM_N], F32R, narrow)
        nw_l = sb("nw_l", [P, KT * SM_N + P - SM_N], F32R, narrow)
        wg2 = sb("wg2", [RANK, GK], F32, narrow)
        narrow.close()
        br_out = ExitStack()
        bo_h = sb("bo_h", [P, 3, BKT, NQ], F32R, br_out)
        bo_l = sb("bo_l", [P, 3, BKT, NQ], F32R, br_out)

        tmp = ExitStack()
        xa = sb("xa", [META, D], F32, tmp)
        xb = sb("xb", [P, 2, D], F32, tmp)
        prow = sb("prow", [P, 5, P], F32, tmp)
        sq1 = sb("sq1", [P, 5, 2, T], F32, tmp)
        tmp.close()
        brt = ExitStack()
        ball = sb("ball", [P, GH, T], F32, brt)
        crow = sb("crow", [FH, T], F32, brt)
        ctok = sb("ctok", [P, 2, FH], F32, brt)
        ctok0 = sb("ctok0", [QM, FH], F32, brt)
        causal = sb("causal", [P, P], F32, brt)
        causal0 = sb("causal0", [QM, META], F32, brt)
        blockd = sb("blockd", [P, T], F32, brt)
        every = sb("every", [P, P + SB], F32, brt)
        lmask = sb("lmask", [P, NA + NB], F32, brt)
        fv = sb("fv", [P, 2, T], F32, brt)
        fk = sb("fk", [P, 2, T], F32, brt)
        fq = sb("fq", [P, 2, T], F32, brt)
        gqk = sb("gqk", [P, 2, T], F32, brt)
        gv = sb("gv", [P, 2, T], F32, brt)
        cneg = sb("cneg", [FH, 2, T], F32, brt)
        vtok = sb("vtok", [P, 2, 2, P], F32, brt)
        vtok0 = sb("vtok0", [META, 2, P], F32, brt)
        nmax = sb("nmax", [P, 2, 3], F32, brt)
        psum_row = sb("psum_row", [P, 2, 3], F32, brt)
        pinv = sb("pinv", [P, 2, 3], F32, brt)
        gates = ExitStack()
        bh = sb("bh", [P, T], F32, gates)
        eb = sb("eb", [P, T], F32, gates)
        gates.close()
        cst = sb("cst", [32 + FH, 2, T], F32R, brt)
        kd = sb("kd", [P, META + P], F32, brt)
        qe = sb("qe", [P, T], F32, brt)
        kdtok = sb("kdtok", [P, P], F32, brt)
        kdtok0 = sb("kdtok0", [META, P], F32, brt)
        gvt = sb("gvt", [P, 2, DV], F32, brt)
        gvt0 = sb("gvt0", [META, DV], F32, brt)
        att = sb("att", [P, T], F32, brt)
        state = sb("state", [P, 2, DV], F32, brt)
        cc, ch = fv[:, :, 0:NC], fk[:, :, 0:NC]
        gr = gv[:, :, 0:NQ]
        on = cy = gqk[:, :, 0:NQ]
        early = ExitStack()
        NTRI = NSB * (SB * (SB + 1) // 2)
        tri = sb("tri", [P, NTRI], F32, early)
        ql = sb("ql", [P, LV, T], F32, early)
        kl = sb("kl", [P, LV, T], F32, early)
        lprod = kl[:].rearrange("p l t -> p (l t)")[:, 0:NA + NB]
        early.close()
        late = ExitStack()
        sc = sb("sc", [P, 2, 432], F32, late)
        pt = sb("pt", [P, 384], F32, late)
        pt0 = sb("pt0", [META, 2 * P + QM], F32, late)
        osq = sb("osq", [P, 2, NQ], F32, late)
        sil = osq
        late.close()
        pro = ExitStack()
        zall = sb("zall", [P, GH, T], F32, pro)
        lall = sb("lall", [P, GH, T], F32, pro)
        pro.close()
        fsc, fmin, flog, glr = fv[0:FH, 0, :], fv[0:FH, 1, :], fk[0:FH, 0, :], fq[0:RANK, 0, :]
        brt.close()
        gtt = ExitStack()
        mix_h = sb("mix_h", [P, KT, NQ], F32R, gtt)
        mix_l = sb("mix_l", [P, KT, NQ], F32R, gtt)
        gate = sb("gate", [P, 3, 2, NQ], F32, gtt)
        mixf = sb("mixf", [P, 2, NQ], F32, gtt)
        mixt = sb("mixt", [P, 2, NQ], F32, gtt)
        osqm = sb("osqm", [P, 2, NQ], F32, gtt)
        gtt.close()
        br_out.close()
        upt = ExitStack()
        act_h = sb("act_h", [P, FT, SEQ], F32R, upt)
        act_l = sb("act_l", [P, FT, SEQ], F32R, upt)
        uu = sb("uu", [P, 2, NQ], F32, upt)
        yg = sb("yg", [P, 2, SEQ], F32, upt)
        yu = sb("yu", [P, 2, SEQ], F32, upt)
        upt.close()
        xn_scope.close()
        ybuf = sb("ybuf", [P, 2, D])
        h3 = sb("h3", [P, 2, SEQ])
        hg = sb("hg", [P, 2, SEQ])
        sq3 = sb("sq3", [P, 2, SEQ])

        landed = [sem(f"landed{s}") for s in range(SLOTS)]
        hi_ready = sem("hi_ready")
        lo_ready = sem("lo_ready")
        panel_used = sem("panel_used")
        set_free = [sem("set0_free"), sem("set1_free")]
        vec = sem("vec")
        x_in = [sem(f"x_in{c}") for c in range(4)]
        g1_in, g1_ps, g1_ok = sem("g1_in"), sem("g1_ps"), sem("g1_ok")
        narrow_in, narrow_hi, narrow_lo = sem("narrow_in"), sem("narrow_hi"), sem("narrow_lo")
        par_in = sem("par_in")
        small_in = sem("small_in")
        sp_turn = sem("sp_turn")
        const_set, mask_step = sem("const_set"), sem("mask_step")
        narrow_zero = sem("narrow_zero")
        par_t = sem("par_t")
        xt_ps, xt_copied, xt_squared, xsq_sum = sem("xt_ps"), sem("xt_copied"), sem("xt_squared"), sem("xsq_sum")
        stat_ps, stat_inv, stat_root, rs1_ready = sem("stat_ps"), sem("stat_inv"), sem("stat_root"), sem("rs1_ready")
        xg_hi, xg_lo = sem("xg_hi"), sem("xg_lo")
        narrow_ps, f_scaled, f_abs = sem("narrow_ps"), sem("f_scaled"), sem("f_abs")
        z_ps, z_abs, z_min, z_exp, z_log, f_log = (sem(n) for n in ("z_ps", "z_abs", "z_min", "z_exp", "z_log", "f_log"))
        gate_ready = sem("gate_ready")
        b_ready = sem("b_ready")
        c_ready, ctok_ps, ctok_copied = sem("c_ready"), sem("ctok_ps"), sem("ctok_copied")
        bh_ready, eb_ready = sem("bh_ready"), sem("eb_ready")
        tri_sub, off_sub, tri_exp, off_exp = sem("tri_sub"), sem("off_sub"), sem("tri_exp"), sem("off_exp")
        off_abs, off_masked = sem("off_abs"), sem("off_masked")
        kd_ready, off_ready, tri_ready, qe_ready = sem("kd_ready"), sem("off_ready"), sem("tri_ready"), sem("qe_ready")
        kd_ps, kdtok_ready, gv_ps, gvt_ready = sem("kd_ps"), sem("kdtok_ready"), sem("gv_ps"), sem("gvt_ready")
        off_ps, tri_ps, st0_ps, st1_ps = sem("off_ps"), sem("tri_ps"), sem("st0_ps"), sem("st1_ps")
        st0_ready, st1_ready, att_ready, go_ps, go_copied = (sem(n) for n in ("st0_ready", "st1_ready", "att_ready", "go_ps", "go_copied"))
        gsq_sum = sem("gsq_sum")
        gstat_ps, gstat_inv, gstat_root = sem("gstat_ps"), sem("gstat_inv"), sem("gstat_root")
        cneg_ready, vt_ps, vtok_ready, score_ps = sem("cneg_ready"), sem("vt_ps"), sem("vtok_ready"), sem("score_ps")
        smax_ready, p_exp, p_ready, pt_ps, pt_copied, pv_ps = (sem(n) for n in ("smax_ready", "p_exp", "p_ready", "pt_ps", "pt_copied", "pv_ps"))
        r_neg, r_exp, oc_full, oc_hi, oa_hi, oa_lo, ob_full, ob_hi, bo_lo = (sem(n) for n in ("r_neg", "r_exp", "oc_full", "oc_hi", "oa_hi", "oa_lo", "ob_full", "ob_hi", "bo_lo"))
        mix_full, mix_hi, mix_lo = sem("mix_full"), sem("mix_hi"), sem("mix_lo")
        h2_hi, h2_lo, h2_squared, h2sq_sum = (sem(n) for n in ("h2_hi", "h2_lo", "h2_squared", "h2sq_sum"))
        r2_ps, r2_step, r2_inv, r2_root = sem("r2_ps"), sem("r2_step"), sem("r2_inv"), sem("r2_root")
        gate_conv, gate_silu, act_full, act_hi, act_lo = (sem(n) for n in ("gate_conv", "gate_silu", "act_full", "act_hi_ok", "act_lo_ok"))
        h3_scaled, h3_squared, yt_ps, yt_copied = (sem(n) for n in ("h3_scaled", "h3_squared", "yt_ps", "yt_copied"))
        sums_done, fst_ps, fst_inv, fst_root, y_scaled, y_out = (sem(n) for n in ("sums_done", "fst_ps", "fst_inv", "fst_root", "y_scaled", "y_out"))

        def panel(buf, s):
            return buf[:, s, :].rearrange("p (j n) -> p j n", j=KJ)

        def tiles(buf, s, j, n):
            return buf[:, s, j * COLS + n * P:j * COLS + (n + 1) * P]

        tri_at = [NSB * sum(SB - u for u in range(r)) for r in range(SB)]

        def tri_r(r):
            return tri[:, tri_at[r]:tri_at[r] + NSB * (SB - r)].rearrange("p (i t) -> p i t", i=NSB)

        def subs(row):
            return row.rearrange("p (i t) -> p i t", t=SB)

        def chunks(row):
            return row[:, META:T].rearrange("p (c t) -> p c t", c=2)

        wi = w_in[0]

        block = ctx.enter_context(nc.Block())

        @block.sync
        def _(sp):
            sp.dma_start(prow[0:KT, 0, :], norm1_g[0].rearrange("(a b) -> a b", b=P)).then_inc(g1_in, 16)
            sp.dma_start(xa[:], meta_tokens).then_inc(g1_in, 16)
            for c in range(4):
                cols = slice(c * KJ * P, (c + 1) * KJ * P)
                sp.dma_start(xb[:, :, cols], x[0, :, cols].rearrange("(b p) n -> p b n", p=P)).then_inc(x_in[c], 16)
            sp.wait_ge(narrow_zero, 1)
            nwk = nw[:, 0:KT * SM_N].rearrange("p (k n) -> p k n", n=SM_N)
            sp.dma_start(nwk[:, :, 0:FH], wi[:, FOX_F:FOX_F + FH].rearrange("(k p) n -> p k n", p=P)).then_inc(narrow_in, 16)
            sp.dma_start(nwk[:, :, SM_LR:SM_LR + RANK],
                         wi[:, GLA_LR:GLA_LR + RANK].rearrange("(k p) n -> p k n", p=P)).then_inc(narrow_in, 16)
            sp.dma_start(wg2[:], gla_w_g2[0]).then_inc(small_in, 16)
            sp.dma_start(bf[:], fox_b_f[0].rearrange("(a b) -> a b", b=1)).then_inc(small_in, 16)
            for at, src, rows in ((N2, norm2_g[0], KT), (NF, final_norm_g, KT),
                                  (GB, gate_b[0], 3 * KT), (GN, gla_norm_g[0], 8), (BG, gla_b_g[0], GH)):
                sp.dma_start(prow[at:at + rows, 0, :], src.rearrange("(a b) -> a b", b=P)).then_inc(par_in, 16)
            sp.dma_start(prow[0:CONV_K * CH // P, 1, :], conv_w[0].rearrange("k (a b) -> (k a) b", b=P)).then_inc(par_in, 16)
            for k in range(CONV_K):
                sp.dma_start(prow[0:2 * FT, 2 + k, :], mlp_conv_w[0, k].rearrange("(a b) -> a b", b=P)).then_inc(par_in, 16)

            def load(ph, i, q, w, k0, col):
                sp.wait_ge(lo_ready, ph.before(i, q))
                if k0 == 0:
                    sp.sem_inc(sp_turn, 1)
                s = ph.slot(q)
                parts = 2 if q < SLOTS else 1
                kts = KJ // parts
                for j in range(0, KJ, kts):
                    sp.dma_start(panel(raw, s)[:, j:j + kts, :],
                                 w[(k0 + j) * P:(k0 + j + kts) * P, bass.ds(col, COLS)].rearrange("(j p) n -> p j n", p=P)
                                 ).then_inc(landed[s], 16)

            with sp.Fori(0, BR.trips) as i:
                for q in range(4):
                    sp.wait_ge(lo_ready, BR.before(i, q))
                    s = BR.slot(q)
                    for n, col in enumerate((GLA_Q, GLA_K)):
                        sp.dma_start(panel(raw, s)[:, :, n * P:(n + 1) * P],
                                     wi[q * KJ * P:(q + 1) * KJ * P, bass.ds(i * P + col, P)]
                                     .rearrange("(j p) n -> p j n", p=P)).then_inc(landed[s], 16)
                for p_, col in enumerate((GLA_V, FOX_V, FOX_K, FOX_Q, GLA_R, SC_C, SC_H, SC_B)):
                    for q in range(4):
                        load(BR, i, 4 * (p_ + 1) + q, wi, q * KJ, i * COLS + col)
            with sp.Fori(0, GT.trips) as i:
                for g in range(3):
                    for q in range(4):
                        load(GT, i, 4 * g + q, wi, q * KJ, i * COLS + (GATES + g * D))
                for g, w in enumerate((w_a_o, w_b_o, w_c_o)):
                    for q in range(2):
                        load(GT, i, 12 + 2 * g + q, w[0], q * KJ, i * COLS)
            with sp.Fori(0, WO.trips) as i:
                for q in range(8):
                    load(WO, i, q, w_o[0], (q % 4) * KJ, i * (2 * COLS) + (q // 4) * COLS)
            with sp.Fori(0, UP.trips) as i:
                for q in range(8):
                    load(UP, i, q, w_up[0], (q % 4) * KJ, i * COLS + (q // 4) * DFF)
            with sp.Fori(0, DN.trips) as i:
                for q in range(22):
                    load(DN, i, q, w_down[0], (q % 11) * KJ, i * (2 * COLS) + (q // 11) * COLS)
            for h in range(YP):
                for b in range(2):
                    sp.wait_ge(y_scaled, 2 * h + b + 1)
                    sp.dma_start(out[0, b * P:(b + 1) * P, h * (D // YP):(h + 1) * (D // YP)],
                                 ybuf[:, b, h * (D // YP):(h + 1) * (D // YP)]).then_inc(y_out, 16)
            sp.wait_ge(y_out, 2 * YP * 16)

        @block.gpsimd
        def _(pool):
            nc.gpsimd.memset(ident[:], 0.0).then_inc(const_set, 1)
            pool.wait_ge(const_set, 1)
            nc.gpsimd.affine_select(out=ident[:], in_=ident[:], compare_op=ALU.not_equal, fill=1.0, base=0,
                                    pattern=[[-1, P]], channel_multiplier=1).then_inc(const_set, 1)
            nc.gpsimd.memset(nw[:], 0.0).then_inc(narrow_zero, 1)
            nc.gpsimd.memset(ones[:], 1.0).then_inc(const_set, 1)
            for pair in range(1, KT // 2 - 2):
                pool.wait_ge(xt_squared, pair + 1)
                if pair > 1:
                    pool.wait_ge(xsq_sum, pair - 1)
                nc.gpsimd.tensor_tensor(sq1[:, 0], sq1[:, 0], sq1[:, 1 + pair % 2], ALU.add).then_inc(xsq_sum, 1)
            pool.wait_ge(rs1_ready, 1)
            pool.wait_ge(set_free[1], 1)
            nc.gpsimd.memset(causal[:], 0.0).then_inc(const_set, 1)
            nc.gpsimd.memset(causal0[:], 0.0).then_inc(const_set, 1)
            nc.gpsimd.memset(lmask[:], 0.0).then_inc(const_set, 1)
            pool.wait_ge(const_set, 6)
            nc.gpsimd.affine_select(out=causal0[:], in_=causal0[:], compare_op=ALU.is_ge, fill=NEG, base=Q0,
                                    pattern=[[-1, META]], channel_multiplier=1)
            nc.gpsimd.affine_select(out=causal[:], in_=causal[:], compare_op=ALU.is_ge, fill=NEG, base=0,
                                    pattern=[[-1, P]], channel_multiplier=1)

            def blocks(row, c, width):
                return row.rearrange("p (c i t) -> p c i t", c=c, t=width)

            masks = [(blocks(blockd[:, 0:META], 1, SB), META // SB, SB, SB),
                     (blocks(blockd[:, META:T], 2, SB), P // SB, SB, SB)]
            for level, at in ((32, 0), (16, NA), (8, NA + 2 * P)):
                right = blocks(lmask[:, at:at + 2 * P], 2, 2 * level)[:, :, :, level:]
                masks.append((right, P // (2 * level), 2 * level, level))
            masks.append((blocks(lmask[:, 2 * P:3 * P], 2, 64), 1, P, 64))
            masks.append((blocks(lmask[:, 3 * P:NA], 1, META)[:, :, :, SB:], 1, META, SB))
            for n, (view, count, step, keys) in enumerate(masks):
                chunks_, width = view.shape[1], view.shape[3]
                nc.gpsimd.memset(view, 1.0).then_inc(mask_step, 1)
                pool.wait_ge(mask_step, 3 * n + 1)
                nc.gpsimd.affine_select(out=view, in_=view, compare_op=ALU.is_ge, fill=0.0, base=0,
                                        pattern=[[0, chunks_], [-step, count], [0, width]], channel_multiplier=1).then_inc(mask_step, 1)
                pool.wait_ge(mask_step, 3 * n + 2)
                nc.gpsimd.affine_select(out=view, in_=view, compare_op=ALU.is_ge, fill=0.0, base=keys - 1,
                                        pattern=[[0, chunks_], [step, count], [0, width]], channel_multiplier=-1).then_inc(mask_step, 1)

        @block.scalar
        def _(act):
            def round_panel(ph, i, q):
                s = ph.slot(q)
                act.wait_ge(landed[s], ph.landed(i, q))
                act.wait_ge(panel_used, ph.before(i, q))
                nc.scalar.copy(hi[:, s, :], raw[:, s, :]).then_inc(hi_ready, 1)

            def pair_done(ph, i, q):
                act.wait_ge(panel_used, ph.panel(i, q) + 1)

            act.sem_inc(hi_ready, SLOTS)
            act.wait_ge(g1_ps, 1)
            nc.scalar.copy(g1[:], ps[:, 2, 0:KT]).then_inc(g1_ok, 1)
            act.wait_ge(g1_ok, 1)
            def square_input(pair):
                act.wait_ge(xt_copied, pair + 1)
                if pair in (3, 4, 5):
                    act.wait_ge(xsq_sum, pair - 2)
                buf = 0 if pair == 0 else 1 + pair % 2 if pair < 6 else pair - 3
                nc.scalar.activation(sq1[:, buf], hT[:, 2 * pair:2 * pair + 2, :], ACT.Square).then_inc(xt_squared, 1)

            def round_input(pair):
                for kt in (2 * pair, 2 * pair + 1):
                    ins = nc.scalar.activation(xh[:, kt, :], hT[:, kt, :], ACT.Copy, scale=g1[:, kt:kt + 1])
                ins.then_inc(xg_hi, 1)

            for pair in range(KT // 2 - 1):
                square_input(pair)
                if pair == KT // 2 - 2:
                    square_input(pair + 1)
                round_input(pair)
                if pair == 3:
                    act.wait_ge(narrow_in, 32)
                    nc.scalar.copy(nw_h[:], nw[:]).then_inc(narrow_hi, 1)
            round_input(KT // 2 - 1)
            for q in range(LOOK):
                round_panel(BR, 0, q)
            act.wait_ge(par_t, 1)
            nc.scalar.copy(par[:, N2:], ps[:, 2, N2:NPAR])
            nc.scalar.copy(cvw[:].rearrange("p k a -> p (k a)"), ps[:, 2, P:P + CONV_K * CH // P])
            nc.scalar.copy(mcw[:].rearrange("p k a -> p (k a)"), ps[:, 3, 0:CONV_K * 2 * FT]).then_inc(set_free[1], 1)
            act.wait_ge(stat_inv, 1)
            nc.scalar.activation(rstd[:], rinv[:], ACT.Sqrt).then_inc(stat_root, 1)
            act.wait_ge(f_scaled, 1)
            act.wait_ge(small_in, 32)
            nc.scalar.activation(flog, fsc, ACT.Abs, bias=bf[:, 0:1]).then_inc(f_abs, 1)
            act.wait_ge(f_abs, 1)
            nc.scalar.activation(flog, flog, ACT.Exp, scale=-1.0).then_inc(z_exp, 1)
            for n, (g0, g1_) in enumerate(((0, 1), (1, GH))):
                act.wait_ge(z_min, g1_)
                for g in range(g0, g1_):
                    ins = nc.scalar.activation(lall[:, g, :], AUX[g][:, 0:T], ACT.Abs, bias=par[:, BG + g:BG + g + 1])
                ins.then_inc(z_abs, 1)
                act.wait_ge(z_abs, n + 1)
                nc.scalar.activation(lall[:, g0:g1_, :], lall[:, g0:g1_, :], ACT.Exp, scale=-1.0).then_inc(z_exp, 1)
            act.wait_ge(z_exp, 2)
            nc.scalar.activation(lall[:, 0:1, :], lall[:, 0:1, :], ACT.Ln, bias=ones[:, 0:1]).then_inc(z_log, 1)
            nc.scalar.activation(flog, flog, ACT.Ln, bias=ones[0:FH, 0:1]).then_inc(f_log, 1)
            act.wait_ge(z_exp, 3)
            nc.scalar.activation(lall[:, 1:GH, :], lall[:, 1:GH, :], ACT.Ln, bias=ones[:, 0:1]).then_inc(z_log, 1)

            with act.Fori(0, BR.trips) as i:
                for q in range(BR.n):
                    round_panel(BR, i, q + LOOK)
                    if q == 0:
                        act.wait_ge(b_ready, i + 1)
                        nc.scalar.activation(bh[:], ball[:, bass.ds(i, 1), :].rearrange("p a t -> p (a t)"),
                                             ACT.Copy, scale=1.0 / 16).then_inc(bh_ready, 1)
                        act.wait_ge(bh_ready, i + 1)
                        nc.scalar.activation(eb[:], bh[:], ACT.Exp).then_inc(eb_ready, 1)
                    if q == 3:
                        act.wait_ge(tri_sub, i + 1)
                        nc.scalar.activation(tri[:], tri[:], ACT.Exp).then_inc(tri_exp, 1)
                    if q == 4:
                        act.wait_ge(off_sub, i + 1)
                        nc.scalar.activation(ql[:, :, META:T], ql[:, :, META:T], ACT.Abs)
                        nc.scalar.activation(ql[:, LV - 1, 0:META], ql[:, LV - 1, 0:META], ACT.Abs).then_inc(off_abs, 1)
                        nc.scalar.activation(kd[:], kd[:], ACT.Exp, scale=-1.0)
                        act.wait_ge(off_abs, i + 1)
                        nc.scalar.activation(ql[:, :, META:T], ql[:, :, META:T], ACT.Exp, scale=-1.0)
                        nc.scalar.activation(ql[:, LV - 1, 0:META], ql[:, LV - 1, 0:META], ACT.Exp, scale=-1.0).then_inc(off_exp, 1)
                    if q == 8:
                        act.wait_ge(kd_ps, i + 1)
                        nc.scalar.copy(kdtok0[:], AUX[0][0:META, 0:P])
                        nc.scalar.copy(kdtok[:], AUX[0][:, P:2 * P]).then_inc(kdtok_ready, 1)
                    if q == 11:
                        act.wait_ge(gv_ps, i + 1)
                        nc.scalar.copy(gvt[:].rearrange("p c v -> p (c v)"), AUX[2][:, 0:2 * DV])
                        nc.scalar.copy(gvt0[:], AUX[3][0:META, 0:DV]).then_inc(gvt_ready, 1)
                    if q == 13:
                        act.wait_ge(st0_ps, i + 1)
                        nc.scalar.copy(state[:, 0, :], AUX[3][:, 0:DV]).then_inc(st0_ready, 1)
                    if q == 15:
                        act.wait_ge(go_ps, i + 1)
                        nc.scalar.activation(osq[:], ps[:, 5:8:2, Q0:T], ACT.Square)
                        for e in range(2):
                            ins = nc.scalar.activation(on[:, e, :], AUX[1 + 2 * e][:, Q0:T], ACT.Copy,
                                                       scale=par[:, bass.ds(i * 2 + (GN + e), 1)])
                        ins.then_inc(go_copied, 1)
                    if q == 17:
                        act.wait_ge(vt_ps, i + 1)
                        nc.scalar.copy(vtok[:].rearrange("p c h d -> p (c h d)"), AUX[2])
                        nc.scalar.copy(vtok0[:].rearrange("p h d -> p (h d)"), AUX[1][0:META, 0:2 * P]).then_inc(vtok_ready, 1)
                    if q == 19:
                        act.wait_ge(gstat_inv, i + 1)
                        nc.scalar.activation(rstd[:, 0:NQ], rinv[:, 0:NQ], ACT.Sqrt).then_inc(gstat_root, 1)
                    if q == 21:
                        act.wait_ge(ctok_ps, i + 1)
                        nc.scalar.copy(ctok[:].rearrange("p b h -> p (b h)"), AUX[2][:, 0:2 * FH])
                        nc.scalar.copy(ctok0[:], AUX[2][0:QM, 2 * FH:3 * FH]).then_inc(ctok_copied, 1)
                    if q in (22, 23):
                        h = q - 22
                        act.wait_ge(smax_ready, i * 2 + (h + 1))
                        for rows, a, b, t in ((P, 0, T, 0), (P, T, T + META + P, 1), (QM, T + META + P, 432, 2)):
                            ins = nc.scalar.activation(sc[0:rows, h, a:b], sc[0:rows, h, a:b], ACT.Exp,
                                                       bias=nmax[0:rows, h, t:t + 1], accum_out=psum_row[0:rows, h, t:t + 1])
                        ins.then_inc(p_exp, 1)
                    if q == 25:
                        act.wait_ge(r_neg, i + 1)
                        nc.scalar.activation(sil[:], sil[:], ACT.Exp).then_inc(r_exp, 1)
                    if q in (26, 28):
                        h = (q - 26) // 2
                        act.wait_ge(pt_ps, i * 2 + (h + 1))
                        if h:
                            act.wait_ge(pv_ps, i * 2 + 1)
                        nc.scalar.copy(pt[:], AUX[0][:, 0:384])
                        nc.scalar.copy(pt0[:], AUX[2][0:META, 0:2 * P + QM]).then_inc(pt_copied, 1)
                    if q == 27:
                        act.wait_ge(oc_full, i + 1)
                        nc.scalar.copy(bo_h[:, 2, bass.ds(i * 2, 2), :], sil[:]).then_inc(oc_hi, 1)
                    if q == 30:
                        act.wait_ge(pv_ps, i * 2 + 2)
                        nc.scalar.copy(bo_h[:, 0, bass.ds(i * 2, 2), :], ps[:, 5:8:2, Q0:T]).then_inc(oa_hi, 1)
                    if q == BR.n - 1:
                        act.wait_ge(ob_full, i + 1)
                        nc.scalar.copy(bo_h[:, 1, bass.ds(i * 2, 2), :], cy).then_inc(ob_hi, 1)

            nc.scalar.activation(warm[:], ones[:, 0:1], ACT.Sigmoid)
            with act.Fori(0, GT.trips) as i:
                for q in range(GT.n):
                    round_panel(GT, i, q + LOOK)
                    if q in (3, 7, 11):
                        g = q // 4
                        act.wait_ge(set_free[g % 2], i * 3 + (GT_SET[g % 2] + (1 + g // 2)))
                        for n in range(2):
                            ins = nc.scalar.activation(gate[:, g, n, :], gate[:, g, n, :], ACT.Sigmoid,
                                                       bias=par[:, bass.ds(i * 2 + (GB + g * KT + n), 1)])
                        ins.then_inc(gate_ready, 1)
                    if q == GT.n - 1:
                        act.wait_ge(mix_full, i + 1)
                        nc.scalar.copy(mix_h[:, bass.ds(i * 2, 2), :], mixf[:]).then_inc(mix_hi, 1)

            with act.Fori(0, WO.trips) as i:
                for q in range(WO.n):
                    round_panel(WO, i, q + LOOK)
                    if q % 4 == 3:
                        pair = q // 4
                        act.wait_ge(set_free[pair], i + (WO_SET[pair] + 1))
                        nc.scalar.activation(osqm[:], hT[:, bass.ds(i * 4 + 2 * pair, 2), Q0:T], ACT.Square).then_inc(h2_squared, 1)
                        for n in range(2):
                            ins = nc.scalar.activation(xh[:, bass.ds(i * 4 + (2 * pair + n), 1), 0:NQ].rearrange("p a t -> p (a t)"),
                                                       hT[:, bass.ds(i * 4 + (2 * pair + n), 1), Q0:T].rearrange("p a t -> p (a t)"),
                                                       ACT.Copy, scale=par[:, bass.ds(i * 4 + (N2 + 2 * pair + n), 1)])
                        ins.then_inc(h2_hi, 1)

            def up_trip(i, first):
                for q in range(UP.n):
                    round_panel(UP, i, q + LOOK)
                    if first and q == 1:
                        act.wait_ge(r2_inv, 1)
                        nc.scalar.activation(rstd[:, 0:NQ], rinv[:, 0:NQ], ACT.Sqrt).then_inc(r2_root, 1)
                    if q == 5:
                        act.wait_ge(gate_conv, i + 1)
                        nc.scalar.activation(yg[:], yg[:], ACT.Silu).then_inc(gate_silu, 1)
                    if q == UP.n - 1:
                        act.wait_ge(act_full, i + 1)
                        nc.scalar.copy(act_h[:, bass.ds(i * 2, 2), :], yu[:]).then_inc(act_hi, 1)

            up_trip(0, True)
            with act.Fori(1, UP.trips) as i:
                up_trip(i, False)

            def down_trip(i, last):
                for q in range(DN.n):
                    if not (last and q + LOOK >= DN.n):
                        round_panel(DN, i, q + LOOK)
                    if last and q == 2:
                        nc.scalar.activation(warm[:], ones[:, 0:1], ACT.Sqrt)
                    if q % 11 == 10:
                        pair = q // 11
                        act.wait_ge(set_free[pair], i + (DN_SET[pair] + 1))
                        nc.scalar.activation(sq3[:], h3[:], ACT.Square).then_inc(h3_squared, 1)
                        for n in range(2):
                            ins = nc.scalar.activation(hg[:, n, :], h3[:, n, :], ACT.Copy,
                                                       scale=par[:, bass.ds(i * 4 + (NF + 2 * pair + n), 1)])
                        ins.then_inc(h3_scaled, 1)

            with act.Fori(0, DN.trips - 1) as i:
                down_trip(i, False)
            down_trip(DN.trips - 1, True)
            act.wait_ge(fst_inv, 1)
            nc.scalar.activation(tokst[:, 2, :], tokst[:, 1, :], ACT.Sqrt).then_inc(fst_root, 1)

        @block.vector
        def _(dve):
            chain = [0, 0, 0]

            def link(ins):
                chain[2] += 1
                ins.then_inc(vec, 1)

            def linked(i):
                dve.wait_ge(vec, i * chain[1] + (chain[0] + chain[2]))

            def trip(per):
                chain[1], chain[2] = per, 0

            def trips_done(trips):
                assert chain[1] == chain[2], chain
                chain[0] += trips * chain[1]
                chain[1] = chain[2] = 0

            def straight_done():
                chain[0] += chain[2]
                chain[2] = 0

            def split_panel(ph, i, q):
                s = ph.slot(q)
                dve.wait_ge(hi_ready, ph.panel(i, q) + 1)
                nc.vector.tensor_tensor(lo[:, s, :], raw[:, s, :], hi[:, s, :].bitcast(F32),
                                        ALU.subtract).then_inc(lo_ready, 1)

            def pair_done(ph, i, q):
                dve.wait_ge(panel_used, ph.panel(i, q) + 1)

            def root_step(i, n):
                link(nc.vector.tensor_tensor(newt[:, 0:n], rstd[:, 0:n], rstd[:, 0:n], ALU.mult))
                linked(i)
                link(nc.vector.scalar_tensor_tensor(out=newt[:, 0:n], in0=newt[:, 0:n], scalar=-0.5, in1=var[:, 0:n],
                                                    op0=ALU.mult, op1=ALU.mult))
                linked(i)
                link(nc.vector.scalar_tensor_tensor(out=rstd[:, 0:n], in0=newt[:, 0:n], scalar=1.5, in1=rstd[:, 0:n],
                                                    op0=ALU.add, op1=ALU.mult))
                linked(i)

            def evacuate(dst, ph, i, q, st, n, a=0):
                pair_done(ph, i, q)
                r = rs1[:, a:a + n].unsqueeze(1).broadcast_to([P, 2, n])
                nc.vector.tensor_tensor(dst, pset(st, n), r, ALU.mult).then_inc(set_free[st], 1)

            nc.vector.memset(ones_r[:].bitcast(F32), 1.0)
            dve.sem_inc(lo_ready, SLOTS)
            trip(0)

            def split_input(pair):
                dve.wait_ge(xg_hi, pair + 1)
                for kt in (2 * pair, 2 * pair + 1):
                    ins = nc.vector.scalar_tensor_tensor(out=xl[:, kt, :], in0=hT[:, kt, :], scalar=g1[:, kt:kt + 1],
                                                         in1=xh[:, kt, :].bitcast(F32), op0=ALU.mult, op1=ALU.subtract)
                ins.then_inc(xg_lo, 1)

            for pair in range(KT // 2):
                dve.wait_ge(xt_ps, pair + 1)
                at = 4 + 2 * (pair % 2)
                nc.vector.tensor_copy(hT[:, 2 * pair:2 * pair + 2, :], ps[:, at:at + 2, 0:T]).then_inc(xt_copied, 1)
                if pair >= 3:
                    split_input(pair - 3)
                if pair == 6:
                    dve.wait_ge(narrow_hi, 1)
                    nc.vector.tensor_tensor(nw_l[:], nw[:], nw_h[:].bitcast(F32), ALU.subtract).then_inc(narrow_lo, 1)
            split_input(5)
            split_input(6)
            split_input(7)
            split_panel(BR, 0, 0)
            dve.wait_ge(stat_ps, 1)
            link(nc.vector.tensor_scalar(var[:], ps[:, 1, 0:T], 1.0 / D, EPS, ALU.mult, ALU.add))
            linked(0)
            nc.vector.reciprocal(rinv[:], var[:]).then_inc(stat_inv, 1)
            dve.wait_ge(stat_root, 1)
            link(nc.vector.tensor_tensor(newt[:], rstd[:], rstd[:], ALU.mult))
            linked(0)
            link(nc.vector.scalar_tensor_tensor(out=newt[:], in0=newt[:], scalar=-0.5, in1=var[:], op0=ALU.mult, op1=ALU.mult))
            linked(0)
            nc.vector.scalar_tensor_tensor(out=rs1[:], in0=newt[:], scalar=1.5, in1=rstd[:],
                                           op0=ALU.add, op1=ALU.mult).then_inc(rs1_ready, 1)
            dve.wait_ge(rs1_ready, 1)
            dve.wait_ge(narrow_ps, 1)
            nc.vector.tensor_tensor(fsc, ps[0:FH, 0, 0:T], rs1[0:FH, :], ALU.mult).then_inc(f_scaled, 1)
            nc.vector.tensor_tensor(glr, ps[SM_LR:SM_LR + RANK, 0, 0:T], rs1[SM_LR:SM_LR + RANK, :],
                                    ALU.mult).then_inc(set_free[0], 1)
            dve.wait_ge(small_in, 32)
            dve.wait_ge(f_scaled, 1)
            link(nc.vector.tensor_scalar(fmin, fsc, bf[:, 0:1], 0.0, ALU.add, ALU.min))
            dve.wait_ge(set_free[1], 1)
            for g in range(GH):
                dve.wait_ge(z_ps, g + 1)
                nc.vector.tensor_scalar(zall[:, g, :], AUX[g][:, 0:T], par[:, BG + g:BG + g + 1], 0.0, ALU.add, ALU.min).then_inc(z_min, 1)
            split_panel(BR, 0, 1)
            nc.vector.memset(psum_row[:], 1.0)
            nc.vector.memset(gqk[:, 0, 0:Q0], 0.0)
            link(nc.vector.memset(every[:], 0.0))
            linked(0)
            link(nc.vector.memset(subs(every[:])[:, :, 0:1], 1.0))
            split_panel(BR, 0, 2)

            def sum_gates(g):
                for a, b in ((0, META), (META, META + P), (META + P, T)):
                    ins = nc.vector.tensor_tensor_scan(ball[:, g, a:b], zall[:, g, a:b], lall[:, g, a:b], 0.0, ALU.add, ALU.subtract)
                ins.then_inc(b_ready, 1)

            dve.wait_ge(z_min, GH)
            dve.wait_ge(z_log, 1)
            sum_gates(0)
            dve.wait_ge(f_log, 1)
            nc.vector.tensor_tensor_scan(crow[:], fmin, flog, 0.0, ALU.add, ALU.subtract).then_inc(c_ready, 1)
            dve.wait_ge(z_log, 2)
            for g in range(1, GH):
                sum_gates(g)
            dve.wait_ge(c_ready, 1)
            dve.wait_ge(mask_step, 21)
            dve.wait_ge(b_ready, GH)
            straight_done()

            with dve.Fori(0, BR.trips) as i:
                trip(27)
                for q in range(BR.n):
                    split_panel(BR, i, q + LOOK)
                    bs, q16, k16 = subs(bh[:]), subs(gqk[:, 0, :]), subs(gqk[:, 1, :])
                    if q == 0:
                        dve.wait_ge(bh_ready, i + 1)
                    if q == 14:
                        dve.wait_ge(st1_ready, i + 1)
                        link(nc.vector.memset(cst[:].bitcast(F32), 0.0))
                        for h in range(2):
                            ins = nc.vector.tensor_scalar(cneg[:, h, :], crow[:], ident[0:FH, bass.ds(i * 2 + h, 1)], -1.0,
                                                          ALU.mult, ALU.mult)
                        link(ins)
                        linked(i)
                        link(nc.vector.tensor_copy(cst[0:FH], cneg[:]))
                        linked(i)
                        nc.vector.tensor_tensor(cst[32:32 + FH], cneg[:], cst[0:FH].bitcast(F32), ALU.subtract).then_inc(cneg_ready, 1)
                    if q < 3:
                        for r in ((0, 1), (2, 3, 4), (5, 6, 7))[q]:
                            ins = nc.vector.tensor_tensor(tri_r(r), bs[:, :, r:SB], bs[:, :, r:r + 1].broadcast_to([P, NSB, SB - r]),
                                                          ALU.subtract)
                        if q == 2:
                            ins.then_inc(tri_sub, 1)
                    if q == 3:
                        for n, level in enumerate(LEVELS):
                            a = 0 if level == META // 2 else META
                            own = bh[:, a:T].rearrange("p (i t) -> p i t", t=2 * level)
                            nc.vector.tensor_tensor(ql[:, n, a:T].rearrange("p (i t) -> p i t", t=2 * level), own,
                                                    own[:, :, level - 1:level].broadcast_to([P, (T - a) // (2 * level), 2 * level]),
                                                    ALU.subtract)
                        nc.vector.tensor_scalar(kd[:, 0:META], bh[:, 0:META], bh[:, META - 1:META], None, ALU.subtract)
                        nc.vector.tensor_scalar(kd[:, META:META + P], bh[:, META:META + P], bh[:, META + P - 1:META + P], None,
                                                ALU.subtract).then_inc(off_sub, 1)
                    if q == 5:
                        dve.wait_ge(set_free[0], i * BR_PER[0] + (BR_SET[0] + 1))
                        dve.wait_ge(off_exp, i + 1)
                        nc.vector.tensor_tensor(kd[:], kd[:], gqk[:, 1, 0:META + P], ALU.mult).then_inc(kd_ready, 1)
                        last8 = ql[:, LV - 1, 0:META]
                        for n, dst in ((1, kl), (0, ql)):
                            ins = nc.vector.tensor_tensor(dst[:, LV - 1, 0:META], last8, gqk[:, n, 0:META], ALU.mult)
                            if n:
                                link(ins)
                            ins = nc.vector.tensor_tensor(dst[:, :, META:T], ql[:, :, META:T],
                                                          gqk[:, n, META:T].unsqueeze(1).broadcast_to([P, LV, 2 * P]), ALU.mult)
                            if n:
                                link(ins)
                                linked(i)
                        ins.then_inc(off_ready, 1)
                        dve.wait_ge(eb_ready, i + 1)
                        nc.vector.tensor_tensor(qe[:], gqk[:, 0, :], eb[:], ALU.mult).then_inc(qe_ready, 1)
                    if q in (6, 7, 8):
                        if q == 6:
                            dve.wait_ge(tri_exp, i + 1)
                        for r in ((0, 1), (2, 3, 4), (5, 6, 7))[q - 6]:
                            ins = nc.vector.tensor_tensor(tri_r(r), tri_r(r), k16[:, :, r:r + 1].broadcast_to([P, NSB, SB - r]), ALU.mult)
                        if q == 8:
                            link(ins)
                    if q in (9, 10, 11):
                        if q == 9:
                            linked(i)
                        for r in ((0, 1), (2, 3, 4), (5, 6, 7))[q - 9]:
                            ins = nc.vector.tensor_tensor(tri_r(r), tri_r(r), q16[:, :, r:SB], ALU.mult)
                        if q == 11:
                            ins.then_inc(tri_ready, 1)
                    if q == 9:
                        dve.wait_ge(off_ps, i + 1)
                        nc.vector.tensor_tensor(lprod[:, 0:NA], AUX[1][:, 0:NA], lmask[:, 0:NA], ALU.mult)
                        nc.vector.tensor_tensor(lprod[:, NA:NA + NB], AUX[2], lmask[:, NA:NA + NB], ALU.mult).then_inc(off_masked, 1)
                    if q == 10:
                        dve.wait_ge(off_masked, i + 1)
                        link(nc.vector.tensor_tensor(lprod[:, 0:2 * P], lprod[:, 0:2 * P], lprod[:, NA:NA + 2 * P], ALU.add))
                        linked(i)
                        link(nc.vector.tensor_tensor(lprod[:, 0:2 * P], lprod[:, 0:2 * P], lprod[:, NA + 2 * P:NA + 4 * P], ALU.add))
                        linked(i)
                        right = lprod[:, 0:2 * P].rearrange("p (c t) -> p c t", c=2)[:, :, 64:]
                        link(nc.vector.tensor_tensor(right, right, lprod[:, 2 * P:3 * P].rearrange("p (c t) -> p c t", c=2), ALU.add))
                    if q == 13:
                        dve.wait_ge(tri_ps, i + 1)
                        link(nc.vector.tensor_tensor(att[:], AUX[0][:, 0:T], blockd[:], ALU.mult))
                        linked(i)
                        nc.vector.tensor_tensor(att[:, 0:META], att[:, 0:META], lprod[:, 3 * P:NA], ALU.add)
                        nc.vector.tensor_tensor(att[:, META:T], att[:, META:T], lprod[:, 0:2 * P], ALU.add).then_inc(att_ready, 1)
                        dve.wait_ge(st0_ready, i + 1)
                        dve.wait_ge(st1_ps, i + 1)
                        nc.vector.scalar_tensor_tensor(out=state[:, 1, :], in0=state[:, 0, :], scalar=eb[:, META + P - 1:META + P],
                                                       in1=AUX[2][:, 0:DV], op0=ALU.mult, op1=ALU.add).then_inc(st1_ready, 1)
                    if q == 16:
                        dve.wait_ge(go_copied, i + 1)
                        nc.vector.tensor_tensor(osq[:, 0, :], osq[:, 0, :], osq[:, 1, :], ALU.add).then_inc(gsq_sum, 1)
                    if q == 18:
                        dve.wait_ge(gstat_ps, i + 1)
                        link(nc.vector.tensor_scalar(var[:, 0:NQ], AUX[0][:, 0:NQ], 1.0 / DV, EPS, ALU.mult, ALU.add))
                        linked(i)
                        nc.vector.reciprocal(rinv[:, 0:NQ], var[:, 0:NQ]).then_inc(gstat_inv, 1)
                    if q == 20:
                        dve.wait_ge(gstat_root, i + 1)
                        root_step(i, NQ)
                        dve.wait_ge(go_copied, i + 1)
                        link(nc.vector.tensor_tensor(on, on, rstd[:, 0:NQ].unsqueeze(1).broadcast_to([P, 2, NQ]), ALU.mult))
                    if q in (21, 22):
                        h = q - 21
                        S = AUX[1 + 2 * h]
                        dve.wait_ge(score_ps, i * 2 + (h + 1))
                        dve.wait_ge(ctok_copied, i + 1)
                        c1, c2 = ctok[:, 0, bass.ds(i * 2 + h, 1)], ctok[:, 1, bass.ds(i * 2 + h, 1)]
                        nc.vector.scalar_tensor_tensor(out=sc[:, h, META + P:T], in0=S[:, META + P:T], scalar=c2, in1=causal[:],
                                                       op0=ALU.add, op1=ALU.add)
                        nc.vector.tensor_scalar(sc[:, h, 0:META + P], S[:, 0:META + P], c2, None, ALU.add)
                        nc.vector.scalar_tensor_tensor(out=sc[:, h, T + META:T + META + P], in0=S[:, T + META:T + META + P], scalar=c1,
                                                       in1=causal[:], op0=ALU.add, op1=ALU.add)
                        nc.vector.tensor_scalar(sc[:, h, T:T + META], S[:, T:T + META], c1, None, ALU.add)
                        link(nc.vector.scalar_tensor_tensor(out=sc[0:QM, h, T + META + P:432], in0=S[0:QM, T + META + P:432],
                                                            scalar=ctok0[:, bass.ds(i * 2 + h, 1)], in1=causal0[:],
                                                            op0=ALU.add, op1=ALU.add))
                        linked(i)
                        for rows, a, b, t in ((P, 0, T, 0), (P, T, T + META + P, 1), (QM, T + META + P, 432, 2)):
                            ins = nc.vector.tensor_reduce(nmax[0:rows, h, t:t + 1], sc[0:rows, h, a:b], AX_X, ALU.max, negate=True)
                        ins.then_inc(smax_ready, 1)
                    if q == 24:
                        for h in range(2):
                            dve.wait_ge(p_exp, i * 2 + (h + 1))
                            link(nc.vector.reciprocal(pinv[:, h, :], psum_row[:, h, :]))
                            linked(i)
                            for rows, a, b, t in ((P, 0, T, 0), (P, T, T + META + P, 1), (QM, T + META + P, 432, 2)):
                                ins = nc.vector.tensor_scalar(sc[0:rows, h, a:b], sc[0:rows, h, a:b], pinv[0:rows, h, t:t + 1],
                                                              None, ALU.mult)
                            ins.then_inc(p_ready, 1)
                        dve.wait_ge(set_free[1], i * BR_PER[1] + (BR_SET[1] + 3))
                        nc.vector.tensor_scalar(sil[:], gr, -1.0, 80.0, ALU.mult, ALU.min).then_inc(r_neg, 1)
                    if q == 26:
                        dve.wait_ge(r_exp, i + 1)
                        link(nc.vector.tensor_scalar(sil[:], sil[:], 1.0, None, ALU.add))
                        linked(i)
                        link(nc.vector.reciprocal(sil[:], sil[:]))
                        link(nc.vector.tensor_tensor(on, on, gr, ALU.mult))
                        linked(i)
                        nc.vector.tensor_tensor(sil[:], sil[:], on, ALU.mult).then_inc(oc_full, 1)
                    if q == 28:
                        dve.wait_ge(oc_hi, i + 1)
                        nc.vector.tensor_tensor(bo_l[:, 2, bass.ds(i * 2, 2), :], sil[:],
                                                bo_h[:, 2, bass.ds(i * 2, 2), :].bitcast(F32), ALU.subtract)
                    if q == 30:
                        dve.wait_ge(oa_hi, i + 1)
                        nc.vector.tensor_tensor(bo_l[:, 0, bass.ds(i * 2, 2), :], ps[:, 5:8:2, Q0:T],
                                                bo_h[:, 0, bass.ds(i * 2, 2), :].bitcast(F32), ALU.subtract).then_inc(oa_lo, 1)
                    if q == 32:
                        dve.wait_ge(set_free[1], i * BR_PER[1] + (BR_SET[1] + 4))
                        dve.wait_ge(set_free[0], i * BR_PER[0] + (BR_SET[0] + 4))
                        link(nc.vector.tensor_tensor(cc, cc, ch, ALU.mult))
                    if q == 33:
                        linked(i)
                        for k in range(CONV_K):
                            for n in range(2):
                                tap = cvw[:, k, bass.ds(i * 2 + n, 1)]
                                if k == 0:
                                    ins = nc.vector.tensor_scalar(cy[:, n, :], cc[:, n, 0:NQ], tap, None, ALU.mult)
                                else:
                                    ins = nc.vector.scalar_tensor_tensor(out=cy[:, n, :], in0=cc[:, n, k:k + NQ], scalar=tap,
                                                                         in1=cy[:, n, :], op0=ALU.mult, op1=ALU.add)
                            link(ins)
                            linked(i)
                    if q == 34:
                        link(nc.vector.tensor_tensor(cy, cy, rs1[:, Q0:T].unsqueeze(1).broadcast_to([P, 2, NQ]), ALU.mult))
                        linked(i)
                    if q == 3:
                        pair_done(BR, i, q)
                        nc.vector.tensor_tensor(gqk[:, 1, :], ps[:, 1, 0:T], rs1[:], ALU.mult)
                        nc.vector.scalar_tensor_tensor(out=gqk[:, 0, Q0:T], in0=ps[:, 0, Q0:T], scalar=float(P) ** -0.5, in1=rs1[:, Q0:T],
                                                       op0=ALU.mult, op1=ALU.mult).then_inc(set_free[0], 1)
                    if q == 19:
                        pair_done(BR, i, q)
                        nc.vector.scalar_tensor_tensor(out=fq[:, :, Q0:T], in0=pset(0, NQ), scalar=float(P) ** -0.5,
                                                       in1=rs1[:, Q0:T].unsqueeze(1).broadcast_to([P, 2, NQ]),
                                                       op0=ALU.mult, op1=ALU.mult).then_inc(set_free[0], 1)
                    if q in (7, 11, 15, 23, 27, 31):
                        dst, a, n = {7: (gv[:], 0, T), 11: (fv[:], 0, T), 15: (fk[:], 0, T), 23: (gr, Q0, NQ),
                                     27: (cc, C0, NC), 31: (ch, C0, NC)}[q]
                        evacuate(dst, BR, i, q, (q // 4) % 2, n, a)
                    if q == BR.n - 1:
                        pair_done(BR, i, q)
                        nc.vector.tensor_tensor(cy, cy, pset(2, NQ), ALU.mult).then_inc(ob_full, 1)
                        dve.wait_ge(ob_hi, i + 1)
                        nc.vector.tensor_tensor(bo_l[:, 1, bass.ds(i * 2, 2), :], cy,
                                                bo_h[:, 1, bass.ds(i * 2, 2), :].bitcast(F32), ALU.subtract).then_inc(bo_lo, 1)
                trips_done(BR.trips)

            with dve.Fori(0, GT.trips) as i:
                trip(1)
                for q in range(GT.n):
                    split_panel(GT, i, q + LOOK)
                    if q in (3, 7, 11):
                        g = q // 4
                        evacuate(gate[:, g], GT, i, q, g % 2, NQ, Q0)
                    if q == 13:
                        dve.wait_ge(gate_ready, i * 3 + 1)
                        pair_done(GT, i, q)
                        nc.vector.tensor_tensor(mixf[:], pset(1, NQ), gate[:, 0], ALU.mult).then_inc(set_free[1], 1)
                    if q == 15:
                        dve.wait_ge(gate_ready, i * 3 + 2)
                        dve.wait_ge(set_free[1], i * 3 + (GT_SET[1] + 2))
                        pair_done(GT, i, q)
                        nc.vector.tensor_tensor(mixt[:], pset(0, NQ), gate[:, 1], ALU.mult).then_inc(set_free[0], 1)
                        dve.wait_ge(gate_ready, i * 3 + 3)
                        dve.wait_ge(set_free[0], i * 3 + (GT_SET[0] + 3))
                        link(nc.vector.tensor_tensor(mixf[:], mixf[:], mixt[:], ALU.add))
                        linked(i)
                    if q == 17:
                        pair_done(GT, i, q)
                        nc.vector.tensor_tensor(mixt[:], pset(1, NQ), gate[:, 2], ALU.mult).then_inc(set_free[1], 1)
                        dve.wait_ge(set_free[1], i * 3 + (GT_SET[1] + 3))
                        nc.vector.tensor_tensor(mixf[:], mixf[:], mixt[:], ALU.add).then_inc(mix_full, 1)
                        dve.wait_ge(mix_hi, i + 1)
                        nc.vector.tensor_tensor(mix_l[:, bass.ds(i * 2, 2), :], mixf[:],
                                                mix_h[:, bass.ds(i * 2, 2), :].bitcast(F32), ALU.subtract).then_inc(mix_lo, 1)
                trips_done(GT.trips)

            link(nc.vector.memset(sqsum[:], 0.0))
            linked(0)
            straight_done()
            with dve.Fori(0, WO.trips) as i:
                for q in range(WO.n):
                    split_panel(WO, i, q + LOOK)
                    if q % 4 == 3:
                        pair = q // 4
                        at = bass.ds(i * 4 + 2 * pair, 2)
                        pair_done(WO, i, q)
                        nc.vector.tensor_tensor(hT[:, at, Q0:T], hT[:, at, Q0:T], pset(pair, NQ), ALU.add).then_inc(set_free[pair], 1)
                        dve.wait_ge(h2_squared, i * 2 + (pair + 1))
                        for n in range(2):
                            nc.vector.tensor_tensor(sqsum[:, 0:NQ], sqsum[:, 0:NQ], osqm[:, n, :], ALU.add).then_inc(h2sq_sum, 1)
                            dve.wait_ge(h2sq_sum, i * 4 + (2 * pair + n + 1))
                        dve.wait_ge(h2_hi, i * 2 + (pair + 1))
                        for n in range(2):
                            one = bass.ds(i * 4 + (2 * pair + n), 1)
                            ins = nc.vector.scalar_tensor_tensor(
                                out=xl[:, one, 0:NQ], in0=hT[:, one, Q0:T], scalar=par[:, bass.ds(i * 4 + (N2 + 2 * pair + n), 1)],
                                in1=xh[:, one, 0:NQ].bitcast(F32), op0=ALU.mult, op1=ALU.subtract)
                        ins.then_inc(h2_lo, 1)

            def up_trip(i, first):
                trip(5)
                for q in range(UP.n):
                    split_panel(UP, i, q + LOOK)
                    if first and q == 1:
                        dve.wait_ge(r2_ps, 1)
                        nc.vector.tensor_scalar(var[:, 0:NQ], AUX[0][:, 0:NQ], 1.0 / D, EPS, ALU.mult, ALU.add).then_inc(r2_step, 1)
                        dve.wait_ge(r2_step, 1)
                        nc.vector.reciprocal(rinv[:, 0:NQ], var[:, 0:NQ]).then_inc(r2_inv, 1)
                    if first and q == 2:
                        dve.wait_ge(r2_root, 1)
                        nc.vector.tensor_tensor(newt[:, 0:NQ], rstd[:, 0:NQ], rstd[:, 0:NQ], ALU.mult).then_inc(r2_step, 1)
                        dve.wait_ge(r2_step, 2)
                        nc.vector.scalar_tensor_tensor(out=newt[:, 0:NQ], in0=newt[:, 0:NQ], scalar=-0.5, in1=var[:, 0:NQ],
                                                       op0=ALU.mult, op1=ALU.mult).then_inc(r2_step, 1)
                        dve.wait_ge(r2_step, 3)
                        nc.vector.scalar_tensor_tensor(out=rstd[:, 0:NQ], in0=newt[:, 0:NQ], scalar=1.5, in1=rstd[:, 0:NQ],
                                                       op0=ALU.add, op1=ALU.mult).then_inc(r2_step, 1)
                        dve.wait_ge(r2_step, 4)
                    if q % 4 == 3:
                        half = q // 4
                        y = yu if half else yg
                        pair_done(UP, i, q)
                        nc.vector.tensor_tensor(uu[:], pset(half, NQ), rstd[:, 0:NQ].unsqueeze(1).broadcast_to([P, 2, NQ]),
                                                ALU.mult).then_inc(set_free[half], 1)
                        dve.wait_ge(set_free[half], i + (UP_SET[half] + 1))
                        for k in range(CONV_K):
                            for n in range(2):
                                tap = mcw[:, k, bass.ds(i * 2 + (half * FT + n), 1)]
                                if k == 0:
                                    ins = nc.vector.tensor_scalar(y[:, n, :], uu[:, n, 0:SEQ], tap, None, ALU.mult)
                                else:
                                    ins = nc.vector.scalar_tensor_tensor(out=y[:, n, :], in0=uu[:, n, k:k + SEQ], scalar=tap,
                                                                         in1=y[:, n, :], op0=ALU.mult, op1=ALU.add)
                            if k == CONV_K - 1 and not half:
                                ins.then_inc(gate_conv, 1)
                            else:
                                link(ins)
                                linked(i)
                    if q == UP.n - 1:
                        dve.wait_ge(gate_silu, i + 1)
                        nc.vector.tensor_tensor(yu[:], yu[:], yg[:], ALU.mult).then_inc(act_full, 1)
                        dve.wait_ge(act_hi, i + 1)
                        nc.vector.tensor_tensor(act_l[:, bass.ds(i * 2, 2), :], yu[:],
                                                act_h[:, bass.ds(i * 2, 2), :].bitcast(F32), ALU.subtract).then_inc(act_lo, 1)

            up_trip(0, True)
            with dve.Fori(1, UP.trips) as i:
                up_trip(i, False)
            trips_done(UP.trips)

            link(nc.vector.memset(sqsum[:], 0.0))
            linked(0)
            straight_done()

            def copy_rows(pair, i, count):
                dve.wait_ge(yt_ps, count)
                nc.vector.tensor_copy(ybuf[:, :, bass.ds(i * (2 * COLS) + pair * COLS, COLS)],
                                      AUX[pair].rearrange("p (b n) -> p b n", b=2)).then_inc(yt_copied, 1)

            def down_trip(i, first, last):
                trip(1 if last else 4)
                for q in range(DN.n):
                    if not (last and q + LOOK >= DN.n):
                        split_panel(DN, i, q + LOOK)
                    if q == 4 and not first:
                        copy_rows(1, i - 1, i * 2)
                    if q == 15:
                        copy_rows(0, i, i * 2 + 1)
                    if q % 11 == 10:
                        pair = q // 11
                        pair_done(DN, i, q)
                        nc.vector.tensor_tensor(h3[:], hT[:, bass.ds(i * 4 + 2 * pair, 2), META:T], pset(pair, SEQ),
                                                ALU.add).then_inc(set_free[pair], 1)
                        if last and pair:
                            break
                        dve.wait_ge(h3_squared, i * 2 + (pair + 1))
                        for n in range(2):
                            ins = nc.vector.tensor_tensor(sqsum[:, 0:SEQ], sqsum[:, 0:SEQ], sq3[:, n, :], ALU.add)
                            if last and n:
                                ins.then_inc(sums_done, 1)
                            else:
                                link(ins)
                                linked(0 if last else i)

            down_trip(0, True, False)
            with dve.Fori(1, DN.trips - 1) as i:
                down_trip(i, False, False)
            trips_done(DN.trips - 1)
            down_trip(DN.trips - 1, False, True)
            trips_done(1)
            dve.wait_ge(fst_ps, 1)
            link(nc.vector.tensor_scalar(tokst[:, 0, :], ps[:, 6:8, 0], 1.0 / D, EPS, ALU.mult, ALU.add))
            linked(0)
            nc.vector.reciprocal(tokst[:, 1, :], tokst[:, 0, :]).then_inc(fst_inv, 1)
            dve.wait_ge(fst_root, 1)
            link(nc.vector.tensor_tensor(tokst[:, 3, :], tokst[:, 2, :], tokst[:, 2, :], ALU.mult))
            linked(0)
            link(nc.vector.scalar_tensor_tensor(out=tokst[:, 3, :], in0=tokst[:, 3, :], scalar=-0.5, in1=tokst[:, 0, :],
                                                op0=ALU.mult, op1=ALU.mult))
            linked(0)
            link(nc.vector.scalar_tensor_tensor(out=tokst[:, 2, :], in0=tokst[:, 3, :], scalar=1.5, in1=tokst[:, 2, :],
                                                op0=ALU.add, op1=ALU.mult))
            linked(0)
            dve.wait_ge(yt_copied, 2 * DN.trips - 1)
            for h in range(YP):
                if h == YP - 1:
                    copy_rows(1, DN.trips - 1, 2 * DN.trips)
                    dve.wait_ge(yt_copied, 2 * DN.trips)
                for b in range(2):
                    part = ybuf[:, b, h * (D // YP):(h + 1) * (D // YP)]
                    nc.vector.tensor_scalar(part, part, tokst[:, 2, b:b + 1], None, ALU.mult).then_inc(y_scaled, 1)

        @block.tensor
        def _(pe):
            def use_panel(ph, i, q, st, moving, n, first, last, skip=0):
                pe.wait_ge(lo_ready, ph.panel(i, q) + 1)
                s = ph.slot(q)
                for m in range(2):
                    a = 0 if m else skip
                    acc = pset(st, n)[:, m, a:]
                    for j in range(KJ):
                        mh, ml = (t[:, a:] for t in moving(j))
                        w_hi, w_lo = tiles(hi, s, j, m), tiles(lo, s, j, m)
                        nc.tensor.matmul(acc, w_hi, mh, start=first and j == 0, stop=False)
                        nc.tensor.matmul(acc, w_hi, ml, start=False, stop=False)
                        ins = nc.tensor.matmul(acc, w_lo, mh, start=False, stop=last and j == KJ - 1)
                ins.then_inc(panel_used, 1)

            def x_window(kt0, a, n):
                return lambda j: (xh[:, kt0 + j, a:a + n], xl[:, kt0 + j, a:a + n])

            pe.sem_inc(panel_used, SLOTS)

            def use_narrow(c):
                pe.wait_ge(xg_lo, 2 * (c + 1))
                pe.wait_ge(narrow_lo, 1)
                for kt in range(KJ * c, KJ * (c + 1)):
                    cols = slice(kt * SM_N, kt * SM_N + P)
                    nc.tensor.matmul(ps[:, 0, 0:T], nw_h[:, cols], xh[:, kt, :], start=kt == 0, stop=False)
                    nc.tensor.matmul(ps[:, 0, 0:T], nw_h[:, cols], xl[:, kt, :], start=False, stop=False)
                    ins = nc.tensor.matmul(ps[:, 0, 0:T], nw_l[:, cols], xh[:, kt, :], start=False, stop=kt == KT - 1)
                if c == 3:
                    ins.then_inc(narrow_ps, 1)

            pe.wait_ge(const_set, 3)
            def keep_warm(n, bank):
                for _ in range(n):
                    nc.tensor.matmul(ps[:, bank, 0:P], ident[:], ident[:], start=True, stop=True)

            keep_warm(8, 3)
            pe.wait_ge(g1_in, 32)
            nc.tensor.transpose(ps[:, 2, 0:KT], prow[0:KT, 0, :], ident[0:KT, 0:KT]).then_inc(g1_ps, 1)
            for pair in range(KT // 2):
                if pair % 2 == 0:
                    pe.wait_ge(x_in[pair // 2], 16)
                if pair >= 2:
                    pe.wait_ge(xt_copied, pair - 1)
                for kt in (2 * pair, 2 * pair + 1):
                    bank = AUX[kt % 4]
                    cols = slice(kt * P, (kt + 1) * P)
                    nc.tensor.transpose(bank[:, 0:META], xa[:, cols], ident[0:META, 0:META])
                    for b in range(2):
                        ins = nc.tensor.transpose(bank[:, META + b * P:META + (b + 1) * P], xb[:, b, cols], ident[:])
                ins.then_inc(xt_ps, 1)
                if pair in (4, 5, 6):
                    keep_warm(3, 3)
            pe.wait_ge(par_in, 144)
            pe.wait_ge(g1_ok, 1)
            nc.tensor.transpose(ps[:, 2, 0:NPAR], prow[0:NPAR, 0, :], ident[0:NPAR, 0:NPAR])
            nconv = CONV_K * CH // P
            nc.tensor.transpose(ps[:, 2, P:P + nconv], prow[0:nconv, 1, :], ident[0:nconv, 0:nconv])
            for k in range(CONV_K):
                ins = nc.tensor.transpose(ps[:, 3, k * 2 * FT:(k + 1) * 2 * FT], prow[0:2 * FT, 2 + k, :], ident[0:2 * FT, 0:2 * FT])
            ins.then_inc(par_t, 1)
            keep_warm(8, 1)
            use_narrow(0)
            pe.wait_ge(xsq_sum, KT // 2 - 3)
            pe.wait_ge(xt_squared, KT // 2)
            for m, buf in enumerate((0, 3, 4)):
                for n in range(2):
                    ins = nc.tensor.matmul(ps[:, 1, 0:T], ones[:], sq1[:, buf, n, :], start=m + n == 0, stop=m + n == 3)
            ins.then_inc(stat_ps, 1)
            for c in range(1, 4):
                use_narrow(c)
            pe.wait_ge(set_free[0], 1)
            pe.wait_ge(small_in, 32)
            pe.wait_ge(xt_copied, KT // 2)
            for g in range(GH):
                nc.tensor.matmul(AUX[g][:, 0:T], wg2[:, g * P:(g + 1) * P], glr, start=True, stop=True).then_inc(z_ps, 1)

            def gla_state_parts(i, q):
                if q == 7:
                    pe.wait_ge(kd_ready, i + 1)
                    nc.tensor.transpose(AUX[0][0:META, 0:P], kd[:, 0:META], ident[:])
                    nc.tensor.transpose(AUX[0][:, P:2 * P], kd[:, META:META + P], ident[:]).then_inc(kd_ps, 1)
                if q == 8:
                    pe.wait_ge(off_ready, i + 1)
                    for n, bank, at, skip in ((1, 1, 0, 0), (0, 1, 2 * P, 64), (2, 2, 0, 0), (3, 2, 2 * P, 0)):
                        for c in range(2):
                            tok = META + c * P
                            w = P - skip
                            nc.tensor.matmul(AUX[bank][:, at + c * w:at + (c + 1) * w], kl[:, n, tok:tok + P],
                                             ql[:, n, tok + skip:tok + P], start=True, stop=True)
                    nc.tensor.matmul(AUX[1][:, 3 * P:NA], kl[:, LV - 1, 0:P], ql[:, LV - 1, 0:META], start=True,
                                     stop=True).then_inc(off_ps, 1)
                if q == 10:
                    pe.wait_ge(off_masked, i + 1)
                    pe.wait_ge(set_free[1], i * BR_PER[1] + (BR_SET[1] + 1))
                    for e in range(2):
                        for c in range(2):
                            nc.tensor.transpose(AUX[2][:, c * DV + e * P:c * DV + (e + 1) * P],
                                                gv[:, e, META + c * P:META + (c + 1) * P], ident[:])
                        ins = nc.tensor.transpose(AUX[3][0:META, e * P:(e + 1) * P], gv[:, e, 0:META], ident[:])
                    ins.then_inc(gv_ps, 1)
                if q == 12:
                    pe.wait_ge(kdtok_ready, i + 1)
                    pe.wait_ge(gvt_ready, i + 1)
                    nc.tensor.matmul(AUX[3][:, 0:DV], kdtok0[:], gvt0[:], start=True, stop=True).then_inc(st0_ps, 1)
                    pe.wait_ge(tri_ready, i + 1)
                    for r in range(SB):
                        ins = nc.tensor.matmul(subs(AUX[0][:, 0:T])[:, :, r:SB], every[:, SB - r:SB - r + P], tri_r(r),
                                               start=(r == 0), stop=(r == SB - 1))
                    ins.then_inc(tri_ps, 1)
                    nc.tensor.matmul(AUX[2][:, 0:DV], kdtok[:], gvt[:, 0, :], start=True, stop=True).then_inc(st1_ps, 1)

            def gla_output(i):
                pe.wait_ge(st1_ready, i + 1)
                pe.wait_ge(att_ready, i + 1)
                pe.wait_ge(qe_ready, i + 1)
                for e in range(2):
                    o = AUX[1 + 2 * e]
                    cols = slice(e * P, (e + 1) * P)
                    ins = nc.tensor.matmul(o[:, 0:META], gvt0[:, cols], att[0:META, 0:META], start=True, stop=True)
                    for c in range(2):
                        tok = slice(META + c * P, META + (c + 1) * P)
                        nc.tensor.matmul(o[:, tok], gvt[:, c, cols], att[:, tok], start=True, stop=False)
                        ins = nc.tensor.matmul(o[:, tok], state[:, c, cols], qe[:, tok], start=False, stop=True)
                ins.then_inc(go_ps, 1)

            def fox_scores(i):
                pe.wait_ge(set_free[0], i * BR_PER[0] + (BR_SET[0] + 3))
                pe.wait_ge(set_free[1], i * BR_PER[1] + (BR_SET[1] + 2))
                pe.wait_ge(cneg_ready, i + 1)
                pe.wait_ge(vtok_ready, i + 1)
                for h in range(2):
                    S = AUX[1 + 2 * h]
                    for at, q_at, keys in ((0, META + P, T), (T, META, META + P)):
                        nc.tensor.matmul(S[:, at:at + keys], fq[:, h, q_at:q_at + P], fk[:, h, 0:keys], start=True, stop=False)
                        nc.tensor.matmul(S[:, at:at + keys], ones_r[:], cst[:, h, 0:keys], start=False, stop=True)
                    at = T + META + P
                    nc.tensor.matmul(S[:, at:at + META], ones_r[:], cst[:, h, 0:META], start=True, stop=False)
                    nc.tensor.matmul(S[:, at:at + META], fq[:, h, Q0:Q0 + P], fk[:, h, 0:META], start=False,
                                     stop=True).then_inc(score_ps, 1)
                for c in range(2):
                    nc.tensor.transpose(AUX[2][:, c * FH:(c + 1) * FH], crow[:, META + c * P:META + (c + 1) * P],
                                        ident[0:FH, 0:FH])
                nc.tensor.transpose(AUX[2][0:QM, 2 * FH:3 * FH], crow[:, Q0:META], ident[0:FH, 0:FH]).then_inc(ctok_ps, 1)

            def fox_transposes(i, h):
                pe.wait_ge(p_ready, i * 2 + (h + 1))
                if h == 0:
                    pe.wait_ge(ctok_copied, i + 1)
                else:
                    pe.wait_ge(pt_copied, i * 2 + 1)
                t1 = T
                nc.tensor.transpose(AUX[0][:, 0:P], sc[:, h, META + P:T], ident[:])
                nc.tensor.transpose(AUX[0][:, P:2 * P], sc[:, h, META:META + P], ident[:])
                nc.tensor.transpose(AUX[0][:, 2 * P:3 * P], sc[:, h, t1 + META:t1 + META + P], ident[:])
                nc.tensor.transpose(AUX[2][0:META, 0:P], sc[:, h, 0:META], ident[:])
                nc.tensor.transpose(AUX[2][0:META, P:2 * P], sc[:, h, t1:t1 + META], ident[:])
                nc.tensor.transpose(AUX[2][0:META, 2 * P:2 * P + QM], sc[0:QM, h, t1 + META + P:t1 + 2 * META + P],
                                    ident[0:QM, 0:QM]).then_inc(pt_ps, 1)

            def fox_output(i, h):
                pe.wait_ge(pt_copied, i * 2 + (h + 1))
                o = AUX[1 + 2 * h]
                nc.tensor.matmul(o[:, META + P:T], vtok[:, 1, h, :], pt[:, 0:P], start=True, stop=False)
                nc.tensor.matmul(o[:, META + P:T], vtok[:, 0, h, :], pt[:, P:2 * P], start=False, stop=False)
                nc.tensor.matmul(o[:, META + P:T], vtok0[:, h, :], pt0[:, 0:P], start=False, stop=True)
                nc.tensor.matmul(o[:, META:META + P], vtok[:, 0, h, :], pt[:, 2 * P:3 * P], start=True, stop=False)
                nc.tensor.matmul(o[:, META:META + P], vtok0[:, h, :], pt0[:, P:2 * P], start=False, stop=True)
                nc.tensor.matmul(o[:, Q0:META], vtok0[:, h, :], pt0[:, 2 * P:2 * P + QM], start=True, stop=True).then_inc(pv_ps, 1)

            window = [(0, T)] * 4 + [(Q0, NQ), (Q0, NQ), (C0, NC), (C0, NC), (Q0, NQ)]
            with pe.Fori(0, BR.trips) as i:
                for q in range(BR.n):
                    pair = q // 4
                    st = pair % 2 if pair < 8 else 2
                    if q % 4 == 0 and pair < 8:
                        pe.wait_ge(set_free[st], i * BR_PER[st] + (BR_SET[st] + pair // 2))
                    if q == 32:
                        pe.wait_ge(oa_lo, i + 1)
                    a, n = window[pair]
                    use_panel(BR, i, q, st, x_window((q % 4) * KJ, a, n), n, q % 4 == 0, q % 4 == 3, 0 if pair else Q0)
                    gla_state_parts(i, q)
                    if q == 14:
                        gla_output(i)
                    if q == 17:
                        pe.wait_ge(gsq_sum, i + 1)
                        nc.tensor.matmul(AUX[0][:, 0:NQ], ones[:], osq[:, 0, :], start=True, stop=True).then_inc(gstat_ps, 1)
                    if q == 16:
                        pe.wait_ge(go_copied, i + 1)
                        pe.wait_ge(set_free[0], i * BR_PER[0] + (BR_SET[0] + 2))
                        for h in range(2):
                            for c in range(2):
                                nc.tensor.transpose(AUX[2][:, (2 * c + h) * P:(2 * c + h + 1) * P],
                                                    fv[:, h, META + c * P:META + (c + 1) * P], ident[:])
                            ins = nc.tensor.transpose(AUX[1][0:META, h * P:(h + 1) * P], fv[:, h, 0:META], ident[:])
                        ins.then_inc(vt_ps, 1)
                    if q == 20:
                        fox_scores(i)
                    if q == 25:
                        fox_transposes(i, 0)
                    if q == 27:
                        fox_transposes(i, 1)
                        fox_output(i, 0)
                    if q == 29:
                        fox_output(i, 1)

            with pe.Fori(0, GT.trips) as i:
                for q in range(GT.n):
                    if q < 12:
                        g, kq = q // 4, q % 4
                        st, before = g % 2, g // 2
                        mv = x_window(kq * KJ, Q0, NQ)
                        last = 3
                    else:
                        g, kq = (q - 12) // 2, q % 2
                        st, before = (g + 1) % 2, 1 + (g + 1) // 2
                        mv = (lambda g, k0: lambda j: (bo_h[:, g, k0 + j, :], bo_l[:, g, k0 + j, :]))(g, kq * KJ)
                        last = 1
                    if kq == 0:
                        pe.wait_ge(set_free[st], i * 3 + (GT_SET[st] + before))
                    if q == 12:
                        pe.wait_ge(bo_lo, BR.trips)
                    use_panel(GT, i, q, st, mv, NQ, kq == 0, kq == last)

            with pe.Fori(0, WO.trips) as i:
                for q in range(WO.n):
                    st, kq = q // 4, q % 4
                    if kq == 0:
                        pe.wait_ge(set_free[st], i + WO_SET[st])
                    pe.wait_ge(mix_lo, 2 * kq + 2)
                    use_panel(WO, i, q, st, (lambda k0: lambda j: (mix_h[:, k0 + j, :], mix_l[:, k0 + j, :]))(kq * KJ),
                              NQ, kq == 0, kq == 3)

            def up_trip(i, first):
                for q in range(UP.n):
                    st, kq = q // 4, q % 4
                    if kq == 0:
                        pe.wait_ge(set_free[st], i + UP_SET[st])
                    if first:
                        pe.wait_ge(h2_lo, 2 * kq + 2)
                    use_panel(UP, i, q, st, x_window(kq * KJ, 0, NQ), NQ, kq == 0, kq == 3)
                    if first and q == 1:
                        pe.wait_ge(h2sq_sum, KT)
                        nc.tensor.matmul(AUX[0][:, 0:NQ], ones[:], sqsum[:, 0:NQ], start=True, stop=True).then_inc(r2_ps, 1)

            up_trip(0, True)
            with pe.Fori(1, UP.trips) as i:
                up_trip(i, False)

            def transpose_rows(pair, count):
                pe.wait_ge(h3_scaled, count)
                if not isinstance(count, int) or count > 1:
                    pe.wait_ge(yt_copied, count - 1)
                for b in range(2):
                    for n in range(2):
                        ins = nc.tensor.transpose(AUX[pair][:, b * COLS + n * P:b * COLS + (n + 1) * P],
                                                  hg[:, n, b * P:(b + 1) * P], ident[:])
                ins.then_inc(yt_ps, 1)

            def down_trip(i, first, last=False):
                for q in range(DN.n):
                    st, kq = q // 11, q % 11
                    if kq == 0:
                        pe.wait_ge(set_free[st], i + DN_SET[st])
                    if first and st == 0:
                        pe.wait_ge(act_lo, 2 * kq + 2)
                    use_panel(DN, i, q, st, (lambda k0: lambda j: (act_h[:, k0 + j, :], act_l[:, k0 + j, :]))(kq * KJ),
                              SEQ, kq == 0, kq == 10)
                    if q == 2 and not first:
                        transpose_rows(1, i * 2)
                    if q == 13:
                        transpose_rows(0, i * 2 + 1)
                    if last and q == 15:
                        pe.wait_ge(sums_done, 1)
                        for b in range(2):
                            nc.tensor.matmul(AUX[2 + b][:, 0:1], sqsum[:, b * P:(b + 1) * P], ones[:, 0:1], start=True, stop=False)

            down_trip(0, True)
            with pe.Fori(1, DN.trips - 1) as i:
                down_trip(i, False)
            down_trip(DN.trips - 1, False, True)
            pe.wait_ge(h3_squared, 2 * DN.trips)
            for n in range(2):
                for b in range(2):
                    ins = nc.tensor.matmul(AUX[2 + b][:, 0:1], sq3[:, n, b * P:(b + 1) * P], ones[:, 0:1], start=False, stop=n == 1)
            ins.then_inc(fst_ps, 1)
            transpose_rows(1, 2 * DN.trips)


_INS = ['x', 'meta_tokens', 'norm1_g', 'w_in', 'fox_b_f', 'gate_b', 'conv_w', 'gla_w_g2', 'gla_b_g', 'gla_norm_g',
        'w_a_o', 'w_b_o', 'w_c_o', 'w_o', 'norm2_g', 'w_up', 'mlp_conv_w', 'w_down', 'final_norm_g']


def kernel(**inputs):
    import numpy as _np
    import concourse.bacc as _bacc
    from concourse import mybir as _mybir
    from concourse.bass_utils import run_bass_kernel_spmd as _run

    nc = _bacc.Bacc("TRN2", target_bir_lowering=False, num_devices=1)
    arrays, args = {}, []
    for name in _INS:
        a = _np.ascontiguousarray(inputs[name])
        arrays[f"in_{name}_dram"] = a
        args.append(nc.dram_tensor(f"in_{name}_dram", a.shape, _mybir.dt.from_np(a.dtype), kind="ExternalInput").ap())
    args.append(nc.dram_tensor("out_dram", inputs['x'].shape, F32, kind="ExternalOutput").ap())
    hybrid_layer(nc, *args)
    r = _run(nc, [arrays], core_ids=[0])
    return r.results[0]["out_dram"]
```
